# Optimizing a Trainium2 kernel written in Bass

```python
import math
import jax
import jax.numpy as jnp
from jax import lax
import numpy as np
import jax, jax.numpy as jnp

D_MODEL = 1024
BATCH = 1
SEQ = 512
DEPTH = 1

GRID_W = 64
CTX_LEN = 256

DN_HEADS = 4
DN_DK = 128
DN_DV = 128
DN_QK = DN_HEADS * DN_DK
DN_WIDTH = DN_HEADS * DN_DV
DN_CONV_DIM = 2 * DN_QK + DN_WIDTH
SHORT_CONV = 7
CHUNK = 64

CF_CH = 512
CF_K = 31

D_MIX = DN_WIDTH + CF_CH
OFF_Z = DN_CONV_DIM
OFF_BA = OFF_Z + DN_WIDTH
OFF_CF = OFF_BA + 4 * DN_HEADS
D_IN = OFF_CF + 2 * CF_CH

N_EXPERTS = 64
TOP_K = 6
N_GROUPS = 8
TOPK_GROUPS = 4
D_EXPERT = 256
D_SHARED = 256
ROUTED_SCALE = 2.5
MOE_BLOCK = 128

EPS = 1e-6


def rmsnorm(x, g):
    xf = x.astype(jnp.float32)
    y = xf * lax.rsqrt(jnp.mean(xf * xf, axis=-1, keepdims=True) + EPS)
    return (y * g.astype(jnp.float32)).astype(x.dtype)

def layernorm(x, g, b):
    xf = x.astype(jnp.float32)
    mu = jnp.mean(xf, axis=-1, keepdims=True)
    var = jnp.mean(jnp.square(xf - mu), axis=-1, keepdims=True)
    y = (xf - mu) * lax.rsqrt(var + EPS) * g.astype(jnp.float32) + b.astype(jnp.float32)
    return y.astype(x.dtype)

def l2norm(x):
    return x * lax.rsqrt(jnp.sum(x * x, axis=-1, keepdims=True) + EPS)

def modulate(h, shift, scale):
    return h * (1 + scale) + shift

def depthwise_conv_seq(x, w):
    k, ch = w.shape
    return lax.conv_general_dilated(x, w[:, None, :].astype(x.dtype), (1,), [(k // 2, k // 2)],
                                    dimension_numbers=('NWC', 'WIO', 'NWC'), feature_group_count=ch)

def depthwise_conv_grid_columns(x, w):
    bsz, n, ch = x.shape
    rows = n // GRID_W
    k = w.shape[0]
    y = lax.conv_general_dilated(x.reshape(bsz, rows, GRID_W, ch), w[:, None, None, :].astype(x.dtype),
                                 (1, 1), [(k // 2, k // 2), (0, 0)],
                                 dimension_numbers=('NHWC', 'HWIO', 'NHWC'), feature_group_count=ch)
    return y.reshape(bsz, n, ch)

def split_mixer_inputs(u):
    return u[..., :OFF_Z], u[..., OFF_Z:OFF_BA], u[..., OFF_BA:OFF_CF], u[..., OFF_CF:]

def delta_inputs(qkv, ba, conv_w, a_log, dt_bias):
    bsz, n, _ = qkv.shape
    qkv = jax.nn.silu(depthwise_conv_seq(qkv, conv_w)).astype(jnp.float32)
    q = l2norm(qkv[..., :DN_QK].reshape(bsz, n, DN_HEADS, DN_DK)) * (DN_DK ** -0.5)
    k = l2norm(qkv[..., DN_QK:2 * DN_QK].reshape(bsz, n, DN_HEADS, DN_DK))
    v = qkv[..., 2 * DN_QK:].reshape(bsz, n, DN_HEADS, DN_DV)
    ba = ba.astype(jnp.float32).reshape(bsz, n, 2, 2, DN_HEADS)
    beta = jax.nn.sigmoid(ba[:, :, :, 0])
    g = -jnp.exp(a_log.astype(jnp.float32)) * jax.nn.softplus(ba[:, :, :, 1] + dt_bias.astype(jnp.float32))
    return q, k, v, beta, g

def gated_delta_chunked(q, k, v, g, beta, s0):
    bsz, n, heads, dk = q.shape
    dv = v.shape[-1]
    nc = n // CHUNK

    def blocks(t):
        t = t.reshape(bsz, nc, CHUNK, heads, *t.shape[3:])
        return jnp.moveaxis(t, (1, 3), (0, 2))

    qc, kc, vc, bc = blocks(q), blocks(k), blocks(v), blocks(beta)
    gc = jnp.cumsum(blocks(g), axis=-1)
    tri_incl = jnp.tril(jnp.ones((CHUNK, CHUNK), dtype=bool))
    tri_strict = jnp.tril(jnp.ones((CHUNK, CHUNK), dtype=bool), -1)
    decay = jnp.exp(jnp.where(tri_incl, gc[..., :, None] - gc[..., None, :], -jnp.inf))
    kb = kc * bc[..., None]
    lmat = jnp.where(tri_strict, jnp.einsum('nbhik,nbhjk->nbhij', kb, kc) * decay, 0.0)
    eye = jnp.eye(CHUNK, dtype=lmat.dtype)
    tinv = lax.linalg.triangular_solve(eye + lmat, jnp.broadcast_to(eye, lmat.shape),
                                       left_side=True, lower=True, unit_diagonal=True)
    u = jnp.einsum('nbhij,nbhjv->nbhiv', tinv, vc * bc[..., None])
    w = jnp.einsum('nbhij,nbhjk->nbhik', tinv, kb * jnp.exp(gc)[..., None])
    intra = jnp.einsum('nbhik,nbhjk->nbhij', qc, kc) * decay
    qd = qc * jnp.exp(gc)[..., None]
    kd = kc * jnp.exp(gc[..., -1:] - gc)[..., None]
    glast = jnp.exp(gc[..., -1])

    def step(s, inp):
        u_i, w_i, a_i, qd_i, kd_i, gl_i = inp
        v_new = u_i - jnp.einsum('bhck,bhkv->bhcv', w_i, s)
        o = jnp.einsum('bhck,bhkv->bhcv', qd_i, s) + jnp.einsum('bhij,bhjv->bhiv', a_i, v_new)
        s = s * gl_i[..., None, None] + jnp.einsum('bhck,bhcv->bhkv', kd_i, v_new)
        return s, o

    s_fin, o = lax.scan(step, s0, (u, w, intra, qd, kd, glast))
    o = jnp.moveaxis(o, (0, 2), (1, 3)).reshape(bsz, n, heads, dv)
    return o, s_fin

def bidir_gated_delta(q, k, v, beta, g, s0_fwd, s0_bwd):
    o_f, s_f = gated_delta_chunked(q, k, v, g[:, :, 0], beta[:, :, 0], s0_fwd)
    fl = lambda t: jnp.flip(t, axis=1)
    o_b, s_b = gated_delta_chunked(fl(q), fl(k), fl(v), fl(g[:, :, 1]), fl(beta[:, :, 1]), s0_bwd)
    return o_f + fl(o_b), s_f, s_b

def gated_head_norm(o, z, norm_g):
    bsz, n = z.shape[0], z.shape[1]
    on = o * lax.rsqrt(jnp.mean(o * o, axis=-1, keepdims=True) + EPS) * norm_g.astype(jnp.float32)
    gate = jax.nn.silu(z.astype(jnp.float32)).reshape(bsz, n, DN_HEADS, DN_DV)
    return (on * gate).reshape(bsz, n, DN_WIDTH).astype(z.dtype)

def conformer_module(cf_in, conv_fn, dw_w, dw_b, ln_g, ln_b):
    y = cf_in[..., :CF_CH] * jax.nn.sigmoid(cf_in[..., CF_CH:])
    y = conv_fn(y, dw_w) + dw_b
    return jax.nn.silu(layernorm(y, ln_g, ln_b))

def swiglu(h, wg, wu, wd):
    return (jax.nn.silu(h @ wg) * (h @ wu)) @ wd

def moe_ffn(h, router_w, router_bias, w_gate, w_up, w_down, s_gate, s_up, s_down):
    bsz, n, d = h.shape
    t = bsz * n
    hf = h.reshape(t, d)
    scores = jax.nn.sigmoid((hf @ router_w).astype(jnp.float32))
    sel = scores + router_bias.astype(jnp.float32)
    grp_score = lax.top_k(sel.reshape(t, N_GROUPS, N_EXPERTS // N_GROUPS), 2)[0].sum(-1)
    _, grp_idx = lax.top_k(grp_score, TOPK_GROUPS)
    grp_keep = jnp.any(grp_idx[..., None] == jnp.arange(N_GROUPS), axis=-2)
    exp_keep = jnp.repeat(grp_keep, N_EXPERTS // N_GROUPS, axis=-1)
    _, top_idx = lax.top_k(jnp.where(exp_keep, sel, -jnp.inf), TOP_K)
    top_w = jnp.take_along_axis(scores, top_idx, axis=-1)
    top_w = top_w / jnp.sum(top_w, axis=-1, keepdims=True) * ROUTED_SCALE
    tk = t * TOP_K
    flat_e = top_idx.reshape(tk)
    order = jnp.argsort(flat_e, stable=True)
    sorted_e = flat_e[order]
    sorted_tok = (order // TOP_K).astype(jnp.int32)
    sorted_w = top_w.reshape(tk)[order]
    counts = jnp.bincount(flat_e, length=N_EXPERTS)
    padded = (counts + MOE_BLOCK - 1) // MOE_BLOCK * MOE_BLOCK
    start = jnp.cumsum(counts) - counts
    pad_end = jnp.cumsum(padded)
    pad_start = pad_end - padded
    dest = pad_start[sorted_e] + jnp.arange(tk) - start[sorted_e]
    n_blocks = -(-tk // MOE_BLOCK) + N_EXPERTS
    n_slots = n_blocks * MOE_BLOCK
    slot_tok = jnp.full((n_slots,), t, jnp.int32).at[dest].set(sorted_tok)
    slot_w = jnp.zeros((n_slots,), jnp.float32).at[dest].set(sorted_w)
    block_exp = jnp.minimum(jnp.searchsorted(pad_end, jnp.arange(n_blocks) * MOE_BLOCK, side='right'),
                            N_EXPERTS - 1)
    h_pad = jnp.concatenate([hf, jnp.zeros((1, d), hf.dtype)], axis=0)

    def expert_block(args):
        tok, e = args
        return swiglu(h_pad[tok], w_gate[e], w_up[e], w_down[e])

    out = lax.map(expert_block, (slot_tok.reshape(n_blocks, MOE_BLOCK), block_exp))
    weighted = (out.reshape(n_slots, d) * slot_w[:, None]).astype(h.dtype)
    routed = jnp.zeros((t + 1, d), h.dtype).at[slot_tok].add(weighted)[:t]
    return (routed + swiglu(hf, s_gate, s_up, s_down)).reshape(bsz, n, d)

def first_inputs(seed: int = 0) -> dict:
    key = jax.random.key(seed)
    ks = jax.random.split(key, 32)
    f32 = jnp.float32
    L = DEPTH

    def nrm(k, shape, s):
        return jax.random.normal(k, shape, f32) * s

    dt = jnp.exp(jax.random.uniform(ks[11], (L, 2, DN_HEADS), f32, math.log(1e-3), math.log(1e-1)))
    return {
        'x': nrm(ks[0], (BATCH, SEQ, D_MODEL), 1.0),
        'c': nrm(ks[1], (BATCH, D_MODEL), 1.0),
        'ctx': nrm(ks[2], (BATCH, CTX_LEN, D_MODEL), 1.0),
        'c_ctx': nrm(ks[3], (D_MODEL,), 1.0),
        'w_mod': nrm(ks[4], (L, D_MODEL, 6 * D_MODEL), 0.5 * D_MODEL ** -0.5),
        'b_mod': nrm(ks[5], (L, 6 * D_MODEL), 0.02),
        'g_mix': 1.0 + nrm(ks[6], (L, D_MODEL), 0.02),
        'g_ffn': 1.0 + nrm(ks[7], (L, D_MODEL), 0.02),
        'w_in': nrm(ks[8], (L, D_MODEL, D_IN), D_MODEL ** -0.5),
        'w_out': nrm(ks[9], (L, D_MIX, D_MODEL), D_MIX ** -0.5),
        'dn_conv_w': nrm(ks[10], (L, SHORT_CONV, DN_CONV_DIM), SHORT_CONV ** -0.5),
        'dn_a_log': jnp.log(jax.random.uniform(ks[12], (L, 2, DN_HEADS), f32, 1.0, 16.0)),
        'dn_dt_bias': dt + jnp.log(-jnp.expm1(-dt)),
        'dn_norm_g': 1.0 + nrm(ks[13], (L, DN_DV), 0.02),
        'cf_dw_w': nrm(ks[14], (L, CF_K, CF_CH), CF_K ** -0.5),
        'cf_dw_b': nrm(ks[15], (L, CF_CH), 0.02),
        'cf_ln_g': 1.0 + nrm(ks[16], (L, CF_CH), 0.02),
        'cf_ln_b': nrm(ks[17], (L, CF_CH), 0.02),
        'router_w': nrm(ks[18], (L, D_MODEL, N_EXPERTS), D_MODEL ** -0.5),
        'router_bias': nrm(ks[19], (L, N_EXPERTS), 0.01),
        'exp_w_gate': nrm(ks[20], (L, N_EXPERTS, D_MODEL, D_EXPERT), D_MODEL ** -0.5),
        'exp_w_up': nrm(ks[21], (L, N_EXPERTS, D_MODEL, D_EXPERT), D_MODEL ** -0.5),
        'exp_w_down': nrm(ks[22], (L, N_EXPERTS, D_EXPERT, D_MODEL), D_EXPERT ** -0.5),
        'sh_w_gate': nrm(ks[23], (L, D_MODEL, D_SHARED), D_MODEL ** -0.5),
        'sh_w_up': nrm(ks[24], (L, D_MODEL, D_SHARED), D_MODEL ** -0.5),
        'sh_w_down': nrm(ks[25], (L, D_SHARED, D_MODEL), D_SHARED ** -0.5),
        'g_final': 1.0 + nrm(ks[26], (D_MODEL,), 0.02),
    }

def first_block(x, c, ctx, c_ctx, w_mod, b_mod, g_mix, g_ffn, w_in, w_out, dn_conv_w, dn_a_log, dn_dt_bias,
              dn_norm_g, cf_dw_w, cf_dw_b, cf_ln_g, cf_ln_b, router_w, router_bias, exp_w_gate, exp_w_up,
              exp_w_down, sh_w_gate, sh_w_up, sh_w_down, g_final):
    bsz = x.shape[0]
    for l in range(DEPTH):
        sh1, sc1, gt1, sh2, sc2, gt2 = jnp.split((jax.nn.silu(c) @ w_mod[l] + b_mod[l])[:, None, :], 6, axis=-1)
        csh1, csc1, cgt1, csh2, csc2, cgt2 = jnp.split(jax.nn.silu(c_ctx) @ w_mod[l] + b_mod[l], 6, axis=-1)

        qkv_c, z_c, ba_c, cf_c = split_mixer_inputs(modulate(rmsnorm(ctx, g_mix[l]), csh1, csc1) @ w_in[l])
        s0 = jnp.zeros((bsz, DN_HEADS, DN_DK, DN_DV), jnp.float32)
        o_c, s_fwd, s_bwd = bidir_gated_delta(
            *delta_inputs(qkv_c, ba_c, dn_conv_w[l], dn_a_log[l], dn_dt_bias[l]), s0, s0)

        qkv_x, z_x, ba_x, cf_x = split_mixer_inputs(modulate(rmsnorm(x, g_mix[l]), sh1, sc1) @ w_in[l])
        o_x, _, _ = bidir_gated_delta(
            *delta_inputs(qkv_x, ba_x, dn_conv_w[l], dn_a_log[l], dn_dt_bias[l]), s_fwd, s_bwd)
        heads_x = jnp.concatenate([
            gated_head_norm(o_x, z_x, dn_norm_g[l]),
            conformer_module(cf_x, depthwise_conv_grid_columns, cf_dw_w[l], cf_dw_b[l], cf_ln_g[l], cf_ln_b[l]),
        ], axis=-1)
        x = x + gt1 * (heads_x @ w_out[l])
        x = x + gt2 * moe_ffn(modulate(rmsnorm(x, g_ffn[l]), sh2, sc2), router_w[l], router_bias[l],
                              exp_w_gate[l], exp_w_up[l], exp_w_down[l], sh_w_gate[l], sh_w_up[l], sh_w_down[l])

        if l + 1 < DEPTH:
            heads_c = jnp.concatenate([
                gated_head_norm(o_c, z_c, dn_norm_g[l]),
                conformer_module(cf_c, depthwise_conv_seq, cf_dw_w[l], cf_dw_b[l], cf_ln_g[l], cf_ln_b[l]),
            ], axis=-1)
            ctx = ctx + cgt1 * (heads_c @ w_out[l])
            ctx = ctx + cgt2 * moe_ffn(modulate(rmsnorm(ctx, g_ffn[l]), csh2, csc2), router_w[l], router_bias[l],
                                       exp_w_gate[l], exp_w_up[l], exp_w_down[l],
                                       sh_w_gate[l], sh_w_up[l], sh_w_down[l])
    return rmsnorm(x, g_final)


DEPTH_2 = 2

HEAD_DIM = 64
D_MIX_2 = D_MODEL
N_GH = 4
GROUP_W = N_GH * HEAD_DIM
IDX_HEADS = 8
IDX_DIM = 64
TOPK_MAX = 256
RET_THETA = 10000.0
GLA_DK = HEAD_DIM // 2
GLA_RANK = 16
GLA_TAU = 16.0
DIFF_DK = HEAD_DIM // 2
ROPE_THETA = 500000.0
ROPE_FRAC = 4
D_FF = 4 * D_MODEL
Q_BLOCK = 128
NEG_INF = -1e30

IN_SPLITS = (
    GROUP_W, HEAD_DIM, HEAD_DIM, IDX_HEADS * IDX_DIM, IDX_DIM, IDX_HEADS,
    GROUP_W, GROUP_W, GROUP_W, GROUP_W,
    N_GH * GLA_DK, N_GH * GLA_DK, GROUP_W, GLA_RANK, GROUP_W,
    2 * N_GH * DIFF_DK, 2 * N_GH * DIFF_DK, GROUP_W,
)
IN_COLS = sum(IN_SPLITS)


def rms_norm(x, g):
    xf = x.astype(jnp.float32)
    y = xf * lax.rsqrt(jnp.mean(xf * xf, axis=-1, keepdims=True) + EPS)
    return (y * g.astype(jnp.float32)).astype(x.dtype)

def head_norm(y, g, center, dtype):
    B, T, H, D = y.shape
    yf = y.astype(jnp.float32)
    if center:
        yf = yf - jnp.mean(yf, axis=-1, keepdims=True)
    yf = yf * lax.rsqrt(jnp.mean(yf * yf, axis=-1, keepdims=True) + EPS)
    yf = yf * g.astype(jnp.float32).reshape(H, D)
    return yf.reshape(B, T, H * D).astype(dtype)

def rope(x, pos, rot_dims, theta):
    half = rot_dims // 2
    inv = theta ** (-jnp.arange(half, dtype=jnp.float32) / half)
    ang = pos.astype(jnp.float32)[..., None] * inv
    cos = jnp.cos(ang)[:, :, None, :].astype(x.dtype)
    sin = jnp.sin(ang)[:, :, None, :].astype(x.dtype)
    x1, x2, xp = x[..., :half], x[..., half:rot_dims], x[..., rot_dims:]
    return jnp.concatenate([x1 * cos - x2 * sin, x1 * sin + x2 * cos, xp], axis=-1)

def split_blocks(a, size):
    B, T = a.shape[:2]
    return jnp.moveaxis(a.reshape((B, T // size, size) + a.shape[2:]), 1, 0)

def merge_blocks(a):
    N, B, S = a.shape[:3]
    return jnp.moveaxis(a, 0, 1).reshape((B, N * S) + a.shape[3:])

def dsa_mixer(q, k, v, qi, ki, wi, pos):
    B, T = q.shape[:2]
    topk = min(TOPK_MAX, T // 4)
    q = rope(q, pos, HEAD_DIM // ROPE_FRAC, ROPE_THETA) * (HEAD_DIM ** -0.5)
    k = rope(k[:, :, None], pos, HEAD_DIM // ROPE_FRAC, ROPE_THETA)[:, :, 0]
    qi = rope(qi, pos, IDX_DIM // ROPE_FRAC, ROPE_THETA)
    ki = rope(ki[:, :, None], pos, IDX_DIM // ROPE_FRAC, ROPE_THETA)[:, :, 0]
    wi = wi * (IDX_HEADS ** -0.5 * IDX_DIM ** -0.5)
    key_chunk = jnp.arange(T) // CHUNK
    gather = jax.vmap(lambda tab, idx: tab[idx])

    def block(args):
        qb, qib, wib, blk = args
        q_chunk = (blk * Q_BLOCK + jnp.arange(Q_BLOCK)) // CHUNK
        admissible = key_chunk[None, :] <= q_chunk[:, None]
        logits = jnp.einsum("bqhd,bsd->bqhs", qib, ki)
        score = jnp.einsum("bqh,bqhs->bqs", wib, jax.nn.relu(logits)).astype(jnp.float32)
        score = jnp.where(admissible[None], score, NEG_INF)
        _, sel = lax.top_k(score, topk)
        valid = (sel // CHUNK) <= q_chunk[None, :, None]
        k_sel = gather(k, sel)
        v_sel = gather(v, sel)
        s = jnp.einsum("bqhd,bqkd->bqhk", qb, k_sel).astype(jnp.float32)
        s = jnp.where(valid[:, :, None, :], s, NEG_INF)
        p = jax.nn.softmax(s, axis=-1).astype(v.dtype)
        return jnp.einsum("bqhk,bqkd->bqhd", p, v_sel)

    out = lax.map(block, (split_blocks(q, Q_BLOCK), split_blocks(qi, Q_BLOCK),
                          split_blocks(wi, Q_BLOCK), jnp.arange(T // Q_BLOCK)))
    return merge_blocks(out)

def retention_mixer(q, k, v, pos):
    B, T, H, D = q.shape
    f32 = jnp.float32
    q = (rope(q, pos, HEAD_DIM, RET_THETA) * (HEAD_DIM ** -0.5)).astype(f32)
    k = rope(k, pos, HEAD_DIM, RET_THETA).astype(f32)
    v = v.astype(f32)
    log_g = jnp.log(1.0 - 2.0 ** (-5.0 - jnp.arange(H, dtype=f32)))
    i = jnp.arange(CHUNK, dtype=f32)
    d_intra = jnp.exp(jnp.abs(i[:, None] - i[None, :])[None] * log_g[:, None, None])
    xi = jnp.exp((i + 1.0)[:, None] * log_g[None, :])[None, :, :, None]
    zeta = jnp.exp((CHUNK - 1.0 - i)[:, None] * log_g[None, :])[None, :, :, None]
    g_chunk = jnp.exp(CHUNK * log_g)[None, :, None, None]

    def step(R, xs):
        qc, kc, vc = xs
        s = jnp.einsum("bihd,bjhd->bhij", qc, kc) * d_intra[None]
        intra = jnp.einsum("bhij,bjhd->bihd", s, vc)
        inter = jnp.einsum("bihd,bhde->bihe", qc, R) * xi
        R = g_chunk * R + jnp.einsum("bjhd,bjhe->bhde", kc * zeta, vc)
        return R, intra + inter

    R0 = jnp.zeros((B, H, D, D), f32)
    _, out = lax.scan(step, R0, (split_blocks(q, CHUNK), split_blocks(k, CHUNK),
                                 split_blocks(v, CHUNK)))
    return merge_blocks(out)

def gla_mixer(q, k, v, a_low, w_a2, b_a):
    B, T, H, DV = v.shape
    f32 = jnp.float32
    log_a = jax.nn.log_sigmoid((jnp.einsum("btr,rk->btk", a_low, w_a2) + b_a).astype(f32)) / GLA_TAU
    log_a = log_a.reshape(B, T, H, GLA_DK)
    q = (q * (GLA_DK ** -0.5)).astype(f32)
    k = k.astype(f32)
    v = v.astype(f32)

    def step(S, xs):
        qc, kc, vc, lac = xs
        b = jnp.cumsum(lac, axis=1)
        decay = jnp.exp(-jnp.abs(b[:, :, None] - b[:, None, :]))
        A = jnp.einsum("bthk,btshk,bshk->bhts", qc, decay, kc)
        intra = jnp.einsum("bhts,bshd->bthd", A, vc)
        inter = jnp.einsum("bthk,bhkd->bthd", qc * jnp.exp(b), S)
        b_last = b[:, -1]
        S = jnp.exp(b_last)[..., None] * S + jnp.einsum(
            "bshk,bshd->bhkd", kc * jnp.exp(b_last[:, None] - b), vc)
        return S, intra + inter

    S0 = jnp.zeros((B, H, GLA_DK, DV), f32)
    _, out = lax.scan(step, S0, (split_blocks(q, CHUNK), split_blocks(k, CHUNK),
                                 split_blocks(v, CHUNK), split_blocks(log_a, CHUNK)))
    return merge_blocks(out)

def diff_mixer(q, k, v, pos, lam_q1, lam_k1, lam_q2, lam_k2, lam_init):
    B, T = q.shape[:2]
    f32 = jnp.float32
    q = rope(q, pos, DIFF_DK // ROPE_FRAC, ROPE_THETA) * (DIFF_DK ** -0.5)
    k = rope(k, pos, DIFF_DK // ROPE_FRAC, ROPE_THETA)
    q = q.reshape(B, T, N_GH, 2, DIFF_DK)
    k = k.reshape(B, T, N_GH, 2, DIFF_DK)
    lam = (jnp.exp(jnp.sum(lam_q1.astype(f32) * lam_k1.astype(f32)))
           - jnp.exp(jnp.sum(lam_q2.astype(f32) * lam_k2.astype(f32))) + lam_init)
    key_chunk = jnp.arange(T) // CHUNK

    def block(args):
        qb, blk = args
        q_chunk = (blk * Q_BLOCK + jnp.arange(Q_BLOCK)) // CHUNK
        mask = key_chunk[None, :] <= q_chunk[:, None]
        s = jnp.einsum("bqhcd,bshcd->bhcqs", qb, k).astype(f32)
        s = jnp.where(mask[None, None, None], s, NEG_INF)
        p = jax.nn.softmax(s, axis=-1)
        w = p[:, :, 0] - lam * p[:, :, 1]
        return jnp.einsum("bhqs,bshd->bqhd", w.astype(v.dtype), v)

    out = lax.map(block, (split_blocks(q, Q_BLOCK), jnp.arange(T // Q_BLOCK)))
    return merge_blocks(out)

def hybrid_layer(x, cond, pos, layer_idx, mod_w, mod_b, attn_pre_g, attn_post_g,
                 mlp_pre_g, mlp_post_g, w_in, gla_wa2, gla_ba, lam_q1, lam_k1,
                 lam_q2, lam_k2, head_norm_g, w_out, mlp_w1, mlp_w2):
    B, T, _ = x.shape
    dt = x.dtype
    mod = (cond @ mod_w + mod_b)[:, None, :]
    shift1, scale1, gate1, shift2, scale2, gate2 = jnp.split(mod, 6, axis=-1)

    h = rms_norm(x, attn_pre_g) * (1.0 + scale1) + shift1
    proj = h @ w_in
    (a_q, a_k, a_v, a_qi, a_ki, a_wi, b_q, b_k, b_v, b_g,
     c_q, c_k, c_v, c_a, c_g, d_q, d_k, d_v) = jnp.split(
        proj, np.cumsum(IN_SPLITS)[:-1].tolist(), axis=-1)
    heads = lambda a, d: a.reshape(B, T, -1, d)
    g_a, g_b, g_c, g_d = jnp.split(head_norm_g, 4)
    lam_init = 0.8 - 0.6 * math.exp(-0.3 * layer_idx)

    y_a = head_norm(dsa_mixer(heads(a_q, HEAD_DIM), a_k, a_v, heads(a_qi, IDX_DIM),
                              a_ki, a_wi, pos), g_a, False, dt)
    y_b = jax.nn.silu(b_g) * head_norm(retention_mixer(
        heads(b_q, HEAD_DIM), heads(b_k, HEAD_DIM), heads(b_v, HEAD_DIM), pos), g_b, True, dt)
    y_c = jax.nn.silu(c_g) * head_norm(gla_mixer(
        heads(c_q, GLA_DK), heads(c_k, GLA_DK), heads(c_v, HEAD_DIM), c_a, gla_wa2, gla_ba),
        g_c, True, dt)
    y_d = head_norm(diff_mixer(heads(d_q, DIFF_DK), heads(d_k, DIFF_DK), heads(d_v, HEAD_DIM),
                               pos, lam_q1, lam_k1, lam_q2, lam_k2, lam_init),
                    g_d, False, dt) * (1.0 - lam_init)
    y = jnp.concatenate([y_a, y_b, y_c, y_d], axis=-1) @ w_out
    x = x + gate1 * rms_norm(y, attn_post_g)

    h = rms_norm(x, mlp_pre_g) * (1.0 + scale2) + shift2
    y = jnp.square(jax.nn.relu(h @ mlp_w1)) @ mlp_w2
    return x + gate2 * rms_norm(y, mlp_post_g)

def second_inputs(seed: int = 0) -> dict:
    key = jax.random.key(seed)
    ks = jax.random.split(key, 20)
    nrm = lambda k, shape, s: jax.random.normal(k, shape, jnp.float32) * s
    gain = lambda k, shape: 1.0 + 0.02 * jax.random.normal(k, shape, jnp.float32)
    x = nrm(ks[0], (BATCH, SEQ, D_MODEL), 1.0)
    c = nrm(ks[1], (BATCH, D_MODEL), 1.0)
    offset = jax.random.randint(ks[2], (BATCH, 1), 0, 64, dtype=jnp.int32) * CHUNK
    positions = offset + jnp.arange(SEQ, dtype=jnp.int32)[None, :]
    return {
        "x": x,
        "c": c,
        "positions": positions,
        "mod_w": nrm(ks[3], (DEPTH_2, D_MODEL, 6 * D_MODEL), 0.5 * D_MODEL ** -0.5),
        "mod_b": nrm(ks[4], (DEPTH_2, 6 * D_MODEL), 0.01),
        "attn_pre_g": gain(ks[5], (DEPTH_2, D_MODEL)),
        "attn_post_g": gain(ks[6], (DEPTH_2, D_MODEL)),
        "mlp_pre_g": gain(ks[7], (DEPTH_2, D_MODEL)),
        "mlp_post_g": gain(ks[8], (DEPTH_2, D_MODEL)),
        "w_in": nrm(ks[9], (DEPTH_2, D_MODEL, IN_COLS), D_MODEL ** -0.5),
        "gla_wa2": nrm(ks[10], (DEPTH_2, GLA_RANK, N_GH * GLA_DK), GLA_RANK ** -0.5),
        "gla_ba": nrm(ks[11], (DEPTH_2, N_GH * GLA_DK), 0.1),
        "lam_q1": nrm(ks[12], (DEPTH_2, DIFF_DK), 0.1),
        "lam_k1": nrm(ks[13], (DEPTH_2, DIFF_DK), 0.1),
        "lam_q2": nrm(ks[14], (DEPTH_2, DIFF_DK), 0.1),
        "lam_k2": nrm(ks[15], (DEPTH_2, DIFF_DK), 0.1),
        "head_norm_g": gain(ks[16], (DEPTH_2, D_MIX_2)),
        "w_out": nrm(ks[17], (DEPTH_2, D_MIX_2, D_MODEL), D_MIX_2 ** -0.5),
        "mlp_w1": nrm(ks[18], (DEPTH_2, D_MODEL, D_FF), D_MODEL ** -0.5),
        "mlp_w2": nrm(ks[19], (DEPTH_2, D_FF, D_MODEL), D_FF ** -0.5),
    }

def second_block(x, c, positions, mod_w, mod_b, attn_pre_g, attn_post_g, mlp_pre_g,
              mlp_post_g, w_in, gla_wa2, gla_ba, lam_q1, lam_k1, lam_q2, lam_k2,
              head_norm_g, w_out, mlp_w1, mlp_w2):
    cond = jax.nn.silu(c)
    for l in range(DEPTH_2):
        x = hybrid_layer(x, cond, positions, l, mod_w[l], mod_b[l], attn_pre_g[l],
                         attn_post_g[l], mlp_pre_g[l], mlp_post_g[l], w_in[l],
                         gla_wa2[l], gla_ba[l], lam_q1[l], lam_k1[l], lam_q2[l],
                         lam_k2[l], head_norm_g[l], w_out[l], mlp_w1[l], mlp_w2[l])
    return x


def setup_inputs(seed=0):
    out = dict(first_inputs(seed))
    for name, value in second_inputs(seed + 1).items():
        if name != "x":
            out[name + "_2"] = value
    return out


def reference(
    x, c, ctx, c_ctx, w_mod, b_mod, g_mix, g_ffn, w_in, w_out, dn_conv_w, dn_a_log, dn_dt_bias,
    dn_norm_g, cf_dw_w, cf_dw_b, cf_ln_g, cf_ln_b, router_w, router_bias, exp_w_gate, exp_w_up,
    exp_w_down, sh_w_gate, sh_w_up, sh_w_down, g_final, c_2, positions_2, mod_w_2, mod_b_2,
    attn_pre_g_2, attn_post_g_2, mlp_pre_g_2, mlp_post_g_2, w_in_2, gla_wa2_2, gla_ba_2,
    lam_q1_2, lam_k1_2, lam_q2_2, lam_k2_2, head_norm_g_2, w_out_2, mlp_w1_2, mlp_w2_2,
):
    x = first_block(
        x, c, ctx, c_ctx, w_mod, b_mod, g_mix, g_ffn, w_in, w_out, dn_conv_w, dn_a_log,
        dn_dt_bias, dn_norm_g, cf_dw_w, cf_dw_b, cf_ln_g, cf_ln_b, router_w, router_bias,
        exp_w_gate, exp_w_up, exp_w_down, sh_w_gate, sh_w_up, sh_w_down, g_final,
    )
    return second_block(
        x, c_2, positions_2, mod_w_2, mod_b_2, attn_pre_g_2, attn_post_g_2, mlp_pre_g_2,
        mlp_post_g_2, w_in_2, gla_wa2_2, gla_ba_2, lam_q1_2, lam_k1_2, lam_q2_2, lam_k2_2,
        head_norm_g_2, w_out_2, mlp_w1_2, mlp_w2_2,
    )


_drawn_inputs = setup_inputs


def setup_inputs(seed=0):
    import zlib

    import numpy as np

    out = dict(_drawn_inputs(seed))
    spreads = {}
    factors = {'c_ctx': 3.892,
     'dn_norm_g': 2.672,
     'cf_ln_g': 2.974,
     'cf_ln_b': 3.465,
     'attn_pre_g_2': 2.794,
     'attn_post_g_2': 5.723,
     'mlp_pre_g_2': 5.631,
     'mlp_post_g_2': 5.83,
     'gla_ba_2': 5.307,
     'lam_q1_2': 5.341,
     'lam_k1_2': 4.022,
     'lam_q2_2': 8.0,
     'lam_k2_2': 6.051,
     'head_norm_g_2': 5.362}
    for name, (base, spread) in spreads.items():
        noise = np.random.default_rng([zlib.crc32(name.encode()), seed]).standard_normal(out[name].shape)
        drawn = base * np.exp(spread * noise) if base else spread * noise
        out[name] = jnp.asarray(drawn.astype(out[name].dtype))
    for name, factor in factors.items():
        out[name] = (out[name] * factor).astype(out[name].dtype)
    return out
```

```python
from contextlib import ExitStack

import numpy as np
import concourse.bass as bass
from concourse import mybir

F32 = mybir.dt.float32
I32 = mybir.dt.int32
U32 = mybir.dt.uint32
ACT = mybir.ActivationFunctionType
ALU = mybir.AluOpType
AX = mybir.AxisListType

P = 128
T = 512
NT = T // P
D = 1024
KD = D // P
EPS = 1e-6
NEG = -1e30
TAKEN = -3e38


class Scope(ExitStack):

    def __init__(self, nc):
        super().__init__()
        self.nc, self.sems = nc, []

    def __exit__(self, *exc):
        super().__exit__(*exc)
        if exc[0] is None:
            self.nc.clear_and_free_semaphores(self.sems)
            self.nc.all_engine_barrier()


class Signal:

    def __init__(self, ctx, nc, name):
        self.sem = nc.alloc_semaphore(name)
        ctx.sems.append(self.sem)
        self.n = 0

    def up(self, by=1):
        self.n += by
        return by


class Turn:

    def __init__(self, nc, ctx, name, banks, ident):
        self.nc, self.banks, self.ident = nc, banks, ident
        self.turned, self.copied = Signal(ctx, nc, name + "_turned"), Signal(ctx, nc, name + "_copied")

    def pe(self, blocks):
        n = self.turned.n
        if n >= len(self.banks):
            self.nc.tensor.wait_ge(self.copied.sem, n - len(self.banks) + 1)
        for src, bank_cols in blocks:
            mm = self.nc.tensor.transpose(self.banks[n % len(self.banks)][0:src.shape[1], bank_cols], src,
                                          self.ident[0:src.shape[0], 0:src.shape[0]])
        mm.then_inc(self.turned.sem, self.turned.up())

    def bank(self, eng):
        n = self.copied.n
        eng.wait_ge(self.turned.sem, n + 1)
        return self.banks[n % len(self.banks)]


class Modulation:
    HALF = 256

    def __init__(self, nc, ctx, name, jobs, slots, acc, rows, bank, ones, out):
        self.nc, self.slots, self.acc, self.rows = nc, slots, acc, rows
        self.bank, self.ones, self.out = bank, ones, out
        self.halves = [(w.rearrange("(k p) n -> p k n", p=P)[:, :, c:c + self.HALF], cond)
                       for w, cond in jobs for c in range(0, w.shape[1], self.HALF)]
        self.tiles = len(self.halves) // 2
        self.loaded = [Signal(ctx, nc, f"{name}_loaded{r}") for r in range(len(slots))]
        self.step, self.scaled, self.reduced, self.copied = (
            Signal(ctx, nc, f"{name}_{s}") for s in ("step", "scaled", "reduced", "copied"))
        self.stored = [Signal(ctx, nc, f"{name}_stored{r}") for r in range(2)]
        self.given, self.product, self.copy = 0, 0, 0

    def load(self, n):
        r = n % len(self.slots)
        if n >= len(self.slots):
            self.nc.gpsimd.wait_ge(self.scaled.sem, n - len(self.slots) + 1)
        self.nc.gpsimd.dma_start(self.slots[r], self.halves[n][0]).then_inc(self.loaded[r].sem, self.loaded[r].up(16))

    def begin(self):
        n, depth = self.given, len(self.slots)
        self.given += 1
        out = self.acc[n // 2 % 2][:, n % 2 * self.HALF:(n % 2 + 1) * self.HALF]
        return n, self.slots[n % depth], self.halves[n][1], out, self.loaded[n % depth], 16 * (n // depth + 1)

    def dve(self):
        dve = self.nc.vector
        n, w, cond, out, landed, value = self.begin()
        dve.wait_ge(landed.sem, value)
        if n % 2 == 0 and n >= 4:
            dve.wait_ge(self.reduced.sem, n // 2 - 1)
        dve.tensor_scalar(out, w[:, 0, :], cond[:, 0:1], None, ALU.mult).then_inc(self.step.sem, self.step.up())
        for k in range(1, KD):
            dve.wait_ge(self.step.sem, self.step.n)
            signal = self.step if k < KD - 1 else self.scaled
            dve.scalar_tensor_tensor(out, w[:, k, :], cond[:, k:k + 1], out, ALU.mult, ALU.add).then_inc(signal.sem, signal.up())

    def pool(self):
        pool, depth = self.nc.gpsimd, len(self.slots)
        for n in range(depth):
            self.load(n)
        for _ in range(2 * self.tiles):
            n, w, cond, out, landed, value = self.begin()
            pool.wait_ge(landed.sem, value)
            if n % 2 == 0 and n >= 4:
                pool.wait_ge(self.reduced.sem, n // 2 - 1)
            c = cond.rearrange("p (k o) -> p k o", o=1).to_broadcast([P, KD, self.HALF])
            pool.tensor_tensor(w, w, c, ALU.mult).then_inc(self.step.sem, self.step.up())
            for m in (4, 2):
                pool.wait_ge(self.step.sem, self.step.n)
                pool.tensor_tensor(w[:, 0:m, :], w[:, 0:m, :], w[:, m:2 * m, :], ALU.add).then_inc(self.step.sem, self.step.up())
            pool.wait_ge(self.step.sem, self.step.n)
            pool.tensor_tensor(out, w[:, 0, :], w[:, 1, :], ALU.add).then_inc(self.scaled.sem, self.scaled.up())
            if n + depth < 2 * self.tiles:
                self.load(n + depth)

    def pe(self):
        n = self.product
        self.product += 1
        pe = self.nc.tensor
        pe.wait_ge(self.scaled.sem, 2 * (n + 1))
        if n >= 1:
            pe.wait_ge(self.copied.sem, n)
        pe.matmul(self.bank, self.ones, self.acc[n % 2], start=True, stop=True).then_inc(self.reduced.sem, self.reduced.up())

    def act(self):
        n = self.copy
        self.copy += 1
        act = self.nc.scalar
        act.wait_ge(self.reduced.sem, n + 1)
        if n >= 2:
            act.wait_ge(self.stored[n % 2].sem, 16 * (n // 2))
        act.activation(self.rows[n % 2], self.bank, ACT.Copy).then_inc(self.copied.sem, self.copied.up())
        act.wait_ge(self.copied.sem, self.copied.n)
        act.dma_start(self.out[n * 512:(n + 1) * 512].rearrange("(a n) -> a n", a=1),
                      self.rows[n % 2]).then_inc(self.stored[n % 2].sem, self.stored[n % 2].up(16))

    def wait_stored(self, eng):
        for r in range(2):
            eng.wait_ge(self.stored[r].sem, 16 * (self.tiles // 2))


NC_ = 256
NCT = NC_ // P
TA = NC_ + T
NTA = TA // P
H1 = 4
TAPS = 7
PAD = TAPS // 2
A_COLS = (0, 512, 1024, 1536, 2048, 2064, 2576, 3088)
GRID = 64
GROWS = T // GRID
CF_TAPS = 31
NTAPS = 2 * GROWS - 1
V_MOD, V_GMIX, V_C, V_CC, V_CFB, V_CONV = 0, 16, 24, 32, 40, 44
INV = 6
AK_ID, AK_TRI, AK_BLK, AK_HALF, AK_ONE, AK_LOW, AK_UP = (n * P for n in (0, 1, 3, 4, 6, 7, 7 + INV))
AK_COLS = (7 + 2 * INV) * P


def mixer_constants():
    c = np.zeros((P, AK_COLS), np.float32)
    i = np.arange(P)
    same = i[:, None] // 64 == i[None] // 64
    c[:, AK_ID:AK_ID + P] = np.eye(P)
    c[:, AK_TRI:AK_TRI + P] = same & (i[:, None] <= i[None])
    c[:, AK_TRI + P:AK_TRI + 2 * P] = same & (i[:, None] >= i[None])
    c[:, AK_BLK:AK_BLK + P] = same
    for o in range(2):
        c[:, AK_HALF + o * P:AK_HALF + (o + 1) * P] = (i // 64 == o)[:, None]
    c[:, AK_ONE:AK_ONE + P] = 1.0
    for l in range(INV):
        blk, half = i >> (l + 1), (i >> l) & 1
        low = (blk[:, None] == blk[None]) & (half[:, None] == 1) & (half[None] == 0)
        c[:, AK_LOW + l * P:AK_LOW + (l + 1) * P] = low
        c[:, AK_UP + l * P:AK_UP + (l + 1) * P] = low.T
    return c


def mixers(nc, x_in, x_out, c, ctx_in, c_ctx, w_mod, b_mod, g_mix, w_in, w_out, conv_w, a_log, dt_bias, norm_g,
           cf_w, cf_b, cf_ln_g, cf_ln_b, c_2, mod_w_2, mod_later, consts):
    pe_, act_, dve_, pool_ = nc.tensor, nc.scalar, nc.vector, nc.gpsimd
    with Scope(nc) as ctx:
        def sb(name, cols, parts=P, dt=F32):
            return ctx.enter_context(nc.sbuf_tensor(f"{name}_a", [parts, cols], dt))

        def sig(name):
            return Signal(ctx, nc, f"{name}_a")

        X = sb("x", NT * D)
        CBW = TA + 4 * PAD
        COW = CBW - 2 * PAD
        AR = sb("arena", KD * TA + H1 * TA + 2 * CBW + 2 * COW)
        ring = sb("ring", 2 * 4096)
        K = sb("consts", AK_COLS)
        QK = sb("kT_qT", H1 * TA + H1 * T)
        TOK = sb("tok", 2 * NTA * 512)
        Z = sb("z", NT * 512)
        CFO = sb("cf_o", 8 * T + NT * 512)
        SQ = sb("squares", 2 * TA)
        ST = sb("states", 2 * 512)
        GB = sb("gateb", D)
        ROW = sb("row", D, parts=1)
        VR, VC = SQ, sb("vcols", 2 * P)
        MC = sb("modcols", 32)
        S = sb("small", 512)
        NG, LG, LB = sb("norm_g", P), sb("ln_g", 512), sb("ln_b", 512)
        PS = ctx.enter_context(nc.psum_tensor("ps_a", [P, 8, 512], F32))

        def part(tile, first, n, **k):
            v = tile[:, first:first + n]
            return v.rearrange("p (a b) -> p a b", **k) if k else v

        x3 = part(X, 0, NT * D, a=NT)
        c3 = part(Z, 0, NCT * D, a=NCT)
        xn = part(TOK, 0, NTA * D, a=NTA)
        hT = part(AR, 0, KD * TA, a=KD)
        vT = part(AR, KD * TA, H1 * TA, a=H1)
        o_ = (KD + H1) * TA
        cb = [part(AR, o_ + n * CBW, CBW) for n in range(2)]
        co = [part(AR, o_ + 2 * CBW + n * COW, COW) for n in range(2)]
        kT, qT = part(QK, 0, H1 * TA, a=H1), part(QK, H1 * TA, H1 * T, a=H1)
        ktok, vtok = part(TOK, 0, NTA * 512, a=NTA), part(TOK, NTA * 512, NTA * 512, a=NTA)
        z3, o3 = part(Z, 0, NT * 512, a=NT), part(CFO, 8 * T, NT * 512, a=NT)
        cy, cc = part(CFO, 0, 4 * T, a=4), part(CFO, 4 * T, 4 * T, a=4)
        cft = part(CFO, 0, NT * 512, a=NT)
        ident, ones = part(K, AK_ID, P), part(K, AK_ONE, P)
        tri = [part(K, AK_TRI + d * P, P) for d in range(2)]
        blk = part(K, AK_BLK, P)
        half_of = [part(K, AK_HALF + o * P, P) for o in range(2)]
        vc, vb = part(VC, 0, P), part(VC, P, P)
        mc = part(MC, 0, 32, b=2)
        ms, rs = S[:, 0:8], S[:, 8:16]
        COND = sb("cond", 48)
        cse_all, cse, cse2, csc, csc2 = COND[:, 0:24], COND[:, 0:16], COND[:, 16:24], COND[:, 24:40], COND[:, 40:48]
        csc_k = csc.rearrange("p (s k) -> p k s", s=2)
        own_v, own_a = sig("dve"), sig("act")

        def heads4(a):
            return a.rearrange("p (h w) -> p h w", h=4)

        def rep(m, n=4):
            return m.rearrange("p (o w) -> p o w", o=1).to_broadcast([P, n, m.shape[1]])

        def cols(w, a, b):
            return w.rearrange("(k p) n -> p k n", p=P)[:, :, a:b]

        W_Q, W_K, W_V, W_Z, W_BA, W_CA, W_CG = range(7)
        order = (W_K, W_V, W_Q, W_Z, W_BA, W_CA, W_CG)
        tiles = [cols(w_mod, t * 512, (t + 1) * 512) for t in range(6)]
        tiles += [cols(w_in, A_COLS[n], A_COLS[n + 1]) for n in order]
        tiles += [w_out[m * 512:(m + 1) * 512, :].rearrange("(k p) n -> p k n", p=P) for m in range(2)]
        slot_of = [0, 1, 2, 3, 0, 1] + [n % 2 for n in range(len(tiles) - 6)]
        before = [max([m for m in range(n) if slot_of[m] == slot_of[n]], default=None) for n in range(len(tiles))]
        w_loaded = [sig(f"w_loaded{r}") for r in range(4)]
        w_used = sig("w_used")
        taken, owed = [0], [False]

        def product(out, lhsT, rhs, start, stop):
            mm = pe_.matmul(out, lhsT, rhs, start=start, stop=stop)
            if owed[0]:
                owed[0] = False
                mm.then_inc(w_used.sem, w_used.up())
            return mm

        def slot(n):
            k, w = tiles[n].shape[1], tiles[n].shape[2]
            r = slot_of[n]
            tile = (ring[:, 0:4096], ring[:, 4096:8192], QK[:, 0:4096], CFO[:, 0:4096])[r]
            return tile[:, 0:k * w].rearrange("p (k n) -> p k n", k=k)

        def loads_of(n):
            return slot_of[:n + 1].count(slot_of[n])

        def take():
            n = taken[0]
            taken[0] += 1
            owed[0] = n > w_used.n
            pe_.wait_ge(w_loaded[slot_of[n]].sem, 16 * loads_of(n))
            return slot(n)

        ld_const, ld_x, ld_ctx, ld_vec, ld_row, ld_bc = (sig(n) for n in ("ld_const", "ld_x", "ld_ctx", "ld_vec", "ld_row", "ld_bc"))
        stored = sig("stored")
        N_VEC, N_BC = 6 + TAPS + 2, 5
        CB2 = NTAPS * 4
        dtb, alog = S[:, 48:56], S[:, 56:64]

        def loads_sp(sp):
            sp.dma_start(K[:, :], consts).then_inc(ld_const.sem, ld_const.up(16))
            sp.dma_start(x3, x_in.rearrange("(t p) d -> p t d", p=P)).then_inc(ld_x.sem, ld_x.up(16))
            sp.dma_start(c3, ctx_in.rearrange("(t p) d -> p t d", p=P)).then_inc(ld_ctx.sem, ld_ctx.up(16))

            def vec(r, src):
                n = src.shape[0] // P
                sp.dma_start(VR[r % P:r % P + n, r // P * P:r // P * P + P], src.rearrange("(r p) -> r p", p=P)).then_inc(ld_vec.sem, ld_vec.up(16))
            for r, src in ((V_MOD, b_mod[0:D]), (V_MOD + 8, b_mod[D:2 * D]), (V_GMIX, g_mix), (V_C, c), (V_CC, c_ctx), (V_CFB, cf_b)):
                vec(r, src)
            for j in range(TAPS):
                vec(V_CONV + 12 * j, conv_w[j, :])
            j0 = CF_TAPS // 2 - (GROWS - 1)
            sp.dma_start(VR[0:NTAPS * 4, P:2 * P], cf_w[j0:j0 + NTAPS, :].rearrange("j (r p) -> (j r) p", p=P)).then_inc(ld_vec.sem, ld_vec.up(16))
            vec(P + CB2, c_2)
            sp.dma_start(ROW[0:1, 0:D], b_mod[2 * D:3 * D].rearrange("(a n) -> a n", a=1)).then_inc(ld_row.sem, ld_row.up(16))

        def loads_act(act):
            for dst, src in ((NG, norm_g), (LG, cf_ln_g), (LB, cf_ln_b)):
                n = src.shape[0]
                act.dma_start(dst[:, :], src.rearrange("(a n) -> a n", a=1).to_broadcast([P, n])).then_inc(ld_bc.sem, ld_bc.up(16))
            for dst, src in ((dtb, dt_bias), (alog, a_log)):
                act.dma_start(dst, src.rearrange("(a d) h -> a (d h)", a=1).to_broadcast([P, 8])).then_inc(ld_bc.sem, ld_bc.up(16))

        vec_turned, vec_cols, silu_e, silu = sig("vec_turned"), sig("vec_cols"), sig("silu_e"), sig("silu")

        def cond_pe():
            pe_.wait_ge(ld_const.sem, 16)
            pe_.wait_ge(ld_vec.sem, 16 * N_VEC)
            pe_.transpose(PS[:, 0, 0:P], VR[:, 0:P], ident)
            pe_.transpose(PS[:, 0, P:P + CB2 + 8], VR[0:CB2 + 8, P:2 * P], ident[0:CB2 + 8, 0:CB2 + 8]).then_inc(vec_turned.sem, vec_turned.up())

        def cond_act():
            act_.wait_ge(vec_cols.sem, 1)
            act_.activation(cse2, vb[:, CB2:CB2 + 8], ACT.Exp, scale=-1.0)
            act_.activation(cse, vc[:, V_C:V_C + 16], ACT.Exp, scale=-1.0).then_inc(silu_e.sem, silu_e.up())

        def cond_dve():
            dve_.wait_ge(vec_turned.sem, 1)
            dve_.tensor_copy(VC[:, 0:P + CB2 + 8], PS[:, 0, 0:P + CB2 + 8]).then_inc(vec_cols.sem, vec_cols.up())
            dve_.wait_ge(silu_e.sem, 1)
            dve_.tensor_scalar(cse_all, cse_all, 1.0, None, ALU.add).then_inc(own_v.sem, own_v.up())
            dve_.wait_ge(own_v.sem, own_v.n)
            dve_.reciprocal(cse_all, cse_all).then_inc(own_v.sem, own_v.up())
            dve_.wait_ge(own_v.sem, own_v.n)
            dve_.tensor_tensor(csc, cse, vc[:, V_C:V_C + 16], ALU.mult).then_inc(silu.sem, silu.up())
            dve_.tensor_tensor(csc2, cse2, vb[:, CB2:CB2 + 8], ALU.mult).then_inc(silu.sem, silu.up())

        mod_mm, gate_mm, mod_cols, gate_row, gb_mm, gb_ready = (sig(n) for n in ("mod_mm", "gate_mm", "mod_cols", "gate_row", "gb_mm", "gb_ready"))

        def mod_pe():
            pe_.wait_ge(silu.sem, 1)
            for t in range(6):
                w = take()
                for k in range(KD):
                    if t < 4:
                        mm = product(PS[0:2, 4 + t, :], csc_k[:, k, :], w[:, k, :], start=k == 0, stop=k == KD - 1)
                    else:
                        mm = product(PS[0:1, t - 2, :], csc[:, k:k + 1], w[:, k, :], start=k == 0, stop=k == KD - 1)
                signal = mod_mm if t < 4 else gate_mm
                mm.then_inc(signal.sem, signal.up())
            pe_.wait_ge(mod_rows.sem, 4)
            for n in range(16):
                mm = pe_.transpose(PS[:, 1, 2 * n:2 * n + 2], MR[0:2, n * P:(n + 1) * P], ident[0:2, 0:2])
            mm.then_inc(mod_turned.sem, mod_turned.up())
            pe_.wait_ge(gate_row.sem, 2)
            for half in range(2):
                mm = pe_.matmul(PS[:, 4 + half, :], ones[0:1, :], ROW[0:1, half * 512:(half + 1) * 512], start=True, stop=True)
            mm.then_inc(gb_mm.sem, gb_mm.up())

        mod_rows, mod_turned = sig("mod_rows"), sig("mod_turned")
        MR = part(CFO, 8 * T, NT * 512)

        def mod_act():
            for t in range(4):
                act_.wait_ge(mod_mm.sem, t + 1)
                act_.activation(MR[0:2, t * 512:(t + 1) * 512], PS[0:2, 4 + t, :], ACT.Copy).then_inc(mod_rows.sem, mod_rows.up())

        def mod_dve():
            dve_.wait_ge(mod_turned.sem, 1)
            ps = PS[:, 1, 0:32].rearrange("p (a b) -> p a b", b=2)
            b16 = vc[:, V_MOD:V_MOD + 16].rearrange("p (a b) -> p a b", b=1).to_broadcast([P, 16, 2])
            g8 = vc[:, V_GMIX:V_GMIX + 8].rearrange("p (a b) -> p a b", b=1).to_broadcast([P, 8, 2])
            dve_.tensor_tensor(mc, ps, b16, ALU.add).then_inc(own_v.sem, own_v.up())
            dve_.wait_ge(own_v.sem, own_v.n)
            dve_.scalar_tensor_tensor(mc[:, 8:16, :], mc[:, 8:16, :], 1.0, g8, ALU.add, ALU.mult).then_inc(mod_cols.sem, mod_cols.up())
            dve_.wait_ge(gate_mm.sem, 2)
            dve_.wait_ge(ld_row.sem, 16)
            for half in range(2):
                g = ROW[0:1, half * 512:(half + 1) * 512]
                dve_.tensor_tensor(g, PS[0:1, 2 + half, :], g, ALU.add).then_inc(gate_row.sem, gate_row.up())
            dve_.wait_ge(gb_mm.sem, 1)
            dve_.tensor_copy(GB[:, :].rearrange("p (b n) -> p b n", b=2), PS[:, 4:6, :]).then_inc(gb_ready.sem, gb_ready.up())

        sq, rs_s, xn_s = sig("sq"), sig("rs"), sig("xn")
        xturn = Turn(nc, ctx, "xturn_a", [PS[:, b, :] for b in (6, 7)], ident)
        cturn = Turn(nc, ctx, "cturn_a", [PS[:, b, :] for b in (4, 5)], ident)

        def square_act():
            act_.wait_ge(ld_ctx.sem, 16)
            act_.wait_ge(ld_x.sem, 16)
            for t in range(NTA):
                src = c3[:, t, :] if t < NCT else x3[:, t - NCT, :]
                act_.activation(AR[:, t * D:(t + 1) * D], src, ACT.Square, accum_out=ms[:, t:t + 1]).then_inc(sq.sem, sq.up())
            act_.wait_ge(sq.sem, NTA)
            act_.activation(rs[:, 0:NTA], ms[:, 0:NTA], ACT.Ln, scale=1.0 / D, bias=EPS).then_inc(own_a.sem, own_a.up())
            act_.wait_ge(own_a.sem, own_a.n)
            act_.activation(rs[:, 0:NTA], rs[:, 0:NTA], ACT.Exp, scale=-0.5).then_inc(rs_s.sem, rs_s.up())

        def norm_act():
            act_.wait_ge(mod_cols.sem, 1)
            for k in range(KD):
                bank = cturn.bank(act_)
                act_.activation(hT[:, k, 0:NC_], bank[:, 0:NC_], ACT.Identity, scale=mc[:, 8 + k, 1:2], bias=mc[:, k, 1:2]).then_inc(cturn.copied.sem, cturn.copied.up())

        def norm_dve():
            dve_.wait_ge(rs_s.sem, 1)
            for t in range(NTA):
                src = c3[:, t, :] if t < NCT else x3[:, t - NCT, :]
                dve_.tensor_scalar(xn[:, t, :], src, rs[:, t:t + 1], None, ALU.mult).then_inc(xn_s.sem, xn_s.up())

        def turned_dve():
            dve_.wait_ge(mod_cols.sem, 1)
            for k in range(KD):
                bank = xturn.bank(dve_)
                dve_.tensor_scalar(hT[:, k, NC_:TA], bank, mc[:, 8 + k, 0:1], mc[:, k, 0:1], ALU.mult, ALU.add).then_inc(xturn.copied.sem, xturn.copied.up())

        def norm_pe():
            pe_.wait_ge(xn_s.sem, NTA)
            for k in range(KD):
                cturn.pe([(xn[:, t, k * P:(k + 1) * P], slice(t * P, (t + 1) * P)) for t in range(NCT)])
                xturn.pe([(xn[:, NCT + t, k * P:(k + 1) * P], slice(t * P, (t + 1) * P)) for t in range(NT)])
            pe_.wait_ge(xturn.copied.sem, KD)
            pe_.wait_ge(cturn.copied.sem, KD)

        later = Modulation(nc, ctx, "later_a", [(w_mod[:, 3 * D:6 * D], csc[:, 0:8]), (mod_w_2, csc2)],
                           [ring[:, r * 2048:(r + 1) * 2048].rearrange("p (k n) -> p k n", k=KD) for r in range(4)],
                           [SQ[:, r * 512:(r + 1) * 512] for r in range(2)],
                           [ROW[0:1, r * 512:(r + 1) * 512] for r in range(2)], PS[0:1, 7, :], ones[:, 0:1], mod_later)
        LATER_LEVELS = (1, 3, 5)

        p_mm, p_ev, cb_zero, conv, conv_silu = sig("p_mm"), sig("p_ev"), sig("cb_zero"), sig("conv"), sig("conv_silu")
        X0 = NC_ + 2 * PAD

        def spans(n):
            return X0 if n >= 8 else 0

        def copies(n):
            return 2 * (n + 1) if n < 8 else n + 9

        def proj_pe():
            for n in range(12):
                if n % 4 == 0:
                    w = take()
                cch = n % 4
                if n >= 2:
                    pe_.wait_ge(p_ev.sem, copies(n - 2))
                for k in range(KD):
                    mm = product(PS[:, (n % 2) * 2, :], w[:, k, cch * P:(cch + 1) * P], hT[:, k, NC_:TA], start=k == 0, stop=k == KD - 1)
                if n < 8:
                    for k in range(KD):
                        mm = product(PS[:, (n % 2) * 2 + 1, 0:NC_], w[:, k, cch * P:(cch + 1) * P], hT[:, k, 0:NC_], start=k == 0, stop=k == KD - 1)
                mm.then_inc(p_mm.sem, p_mm.up())

        def dst(n):
            return (kT, vT, qT)[n // 4][:, n % 4, :]

        def proj_act():
            def silu_of(n):
                act_.wait_ge(conv.sem, n + 1)
                b = co[n % 2]
                if n < 8:
                    act_.activation(dst(n)[:, 0:NC_], b[:, 0:NC_], ACT.Silu)
                    act_.activation(dst(n)[:, NC_:TA], b[:, X0:X0 + T], ACT.Silu).then_inc(conv_silu.sem, conv_silu.up())
                else:
                    act_.activation(dst(n), b[:, X0:X0 + T], ACT.Silu).then_inc(conv_silu.sem, conv_silu.up())
            act_.wait_ge(cb_zero.sem, 2)
            for n in range(12):
                act_.wait_ge(p_mm.sem, n + 1)
                if n >= 2:
                    act_.wait_ge(conv.sem, n - 1)
                b = cb[n % 2]
                act_.activation(b[:, X0 + PAD:X0 + PAD + T], PS[:, (n % 2) * 2, :], ACT.Copy).then_inc(p_ev.sem, p_ev.up())
                if n < 8:
                    act_.activation(b[:, PAD:PAD + NC_], PS[:, (n % 2) * 2 + 1, 0:NC_], ACT.Copy).then_inc(p_ev.sem, p_ev.up())
                if n >= 1:
                    silu_of(n - 1)
            silu_of(11)

        def proj_dve():
            for n in range(2):
                dve_.memset(cb[n], 0.0).then_inc(cb_zero.sem, cb_zero.up())
            for n in range(12):
                dve_.wait_ge(p_ev.sem, copies(n))
                if n >= 2:
                    dve_.wait_ge(conv_silu.sem, n - 1)
                a = spans(n)
                b, o = cb[n % 2], co[n % 2][:, a:COW]
                chunk = (4 + n) % 12 if n < 8 else n - 8
                for j in range(TAPS):
                    tap = vc[:, V_CONV + 12 * j + chunk:V_CONV + 12 * j + chunk + 1]
                    src = b[:, a + j:COW + j]
                    if j == 0:
                        ins = dve_.tensor_scalar(o, src, tap, None, ALU.mult)
                    else:
                        ins = dve_.scalar_tensor_tensor(o, src, tap, o, ALU.mult, ALU.add)
                    signal = conv if j == TAPS - 1 else own_v
                    ins.then_inc(signal.sem, signal.up())
                    dve_.wait_ge(signal.sem, signal.n)

        z_mm, z_ev, ba_mm, ba_ev, cf_mm, cf_ev = (sig(n) for n in ("z_mm", "z_ev", "ba_mm", "ba_ev", "cf_mm", "cf_ev"))
        ba = S[:, 64:160].rearrange("p (t c) -> p t c", t=NTA)

        def rest_pe():
            w = take()
            for t in range(NT):
                if t >= 2:
                    pe_.wait_ge(z_ev.sem, t - 1)
                for k in range(KD):
                    mm = product(PS[:, 4 + t % 2, :], hT[:, k, NC_ + t * P:NC_ + (t + 1) * P], w[:, k, :], start=k == 0, stop=k == KD - 1)
                mm.then_inc(z_mm.sem, z_mm.up())
            w = take()
            for t in range(NTA):
                for k in range(KD):
                    mm = product(PS[:, 6, t * 16:(t + 1) * 16], hT[:, k, t * P:(t + 1) * P], w[:, k, :], start=k == 0, stop=k == KD - 1)
            mm.then_inc(ba_mm.sem, ba_mm.up())
            pe_.wait_ge(p_ev.sem, copies(11))
            for m in range(2):
                w = take()
                if m == 1:
                    pe_.wait_ge(z_ev.sem, NT)
                    pe_.wait_ge(ba_ev.sem, 1)
                for cch in range(4):
                    for k in range(KD):
                        mm = product(PS[:, 4 * m + cch, :], w[:, k, cch * P:(cch + 1) * P], hT[:, k, NC_:TA], start=k == 0, stop=k == KD - 1)
                    mm.then_inc(cf_mm.sem, cf_mm.up())

        def rest_act():
            for t in range(NT):
                act_.wait_ge(z_mm.sem, t + 1)
                act_.activation(z3[:, t, :], PS[:, 4 + t % 2, :], ACT.Copy).then_inc(z_ev.sem, z_ev.up())
            act_.wait_ge(ba_mm.sem, 1)
            act_.activation(S[:, 64:160], PS[:, 6, 0:96], ACT.Copy).then_inc(ba_ev.sem, ba_ev.up())
            for cch in range(4):
                act_.wait_ge(cf_mm.sem, 5 + cch)
                act_.activation(cy[:, cch, :], PS[:, 4 + cch, :], ACT.Exp, scale=-1.0).then_inc(cf_ev.sem, cf_ev.up())

        cf_conv, cf_read = sig("cf_conv"), sig("cf_read")

        def cf_dve():
            for cch in range(4):
                dve_.wait_ge(cf_ev.sem, cch + 1)
                y = cy[:, cch, :]
                dve_.tensor_scalar(y, y, 1.0, None, ALU.add).then_inc(own_v.sem, own_v.up())
                dve_.wait_ge(own_v.sem, own_v.n)
                dve_.reciprocal(y, y).then_inc(own_v.sem, own_v.up())
                dve_.wait_ge(own_v.sem, own_v.n)
                dve_.tensor_tensor(y, y, PS[:, cch, :], ALU.mult).then_inc(cf_read.sem, cf_read.up())
                dve_.wait_ge(cf_read.sem, cf_read.n)
            for cch in range(4):
                y, o = cy[:, cch, :], cc[:, cch, :]
                mid = GROWS - 1
                dve_.tensor_scalar(o, y, vb[:, mid * 4 + cch:mid * 4 + cch + 1], vc[:, V_CFB + cch:V_CFB + cch + 1], ALU.mult, ALU.add).then_inc(own_v.sem, own_v.up())
                dve_.wait_ge(own_v.sem, own_v.n)
                for r in [r for r in range(1 - GROWS, GROWS) if r != 0]:
                    n = (GROWS - abs(r)) * GRID
                    a, b = (0, r * GRID) if r > 0 else (-r * GRID, 0)
                    tap = vb[:, (mid + r) * 4 + cch:(mid + r) * 4 + cch + 1]
                    signal = cf_conv if r == GROWS - 1 else own_v
                    dve_.scalar_tensor_tensor(o[:, a:a + n], y[:, b:b + n], tap, o[:, a:a + n], ALU.mult, ALU.add).then_inc(signal.sem, signal.up())
                    dve_.wait_ge(signal.sem, signal.n)

        l_sq, l_mm, l_rs, l_done, l_ev = sig("l_sq"), sig("l_mm"), sig("l_rs"), sig("l_done"), sig("l_ev")
        sqb = [part(SQ, n * TA, TA) for n in range(2)]
        tturn = Turn(nc, ctx, "tturn_a", [PS[:, b, :] for b in (4, 5, 6, 7)], ident)

        def vec_of(m):
            if m < 4:
                return kT[:, m, :], [(0, NC_), (NC_, TA)]
            return qT[:, m - 4, :], [(0, T)]

        def l2_act():
            for m in range(8):
                v, pieces = vec_of(m)
                n = pieces[-1][1]
                if m >= 2:
                    act_.wait_ge(l_done.sem, m - 1)
                act_.activation(sqb[m % 2][:, 0:n], v, ACT.Square).then_inc(l_sq.sem, l_sq.up())
                act_.wait_ge(l_mm.sem, m + 1)
                for j, (a, b) in enumerate(pieces):
                    act_.activation(sqb[m % 2][:, a:b], PS[:, (m % 2) * 2 + j, 0:b - a], ACT.Ln, bias=EPS).then_inc(l_ev.sem, l_ev.up())
                act_.wait_ge(l_ev.sem, l_ev.n)
                act_.activation(sqb[m % 2][:, 0:n], sqb[m % 2][:, 0:n], ACT.Exp, scale=-0.5,
                                bias=0.0 if m < 4 else -0.5 * float(np.log(P))).then_inc(l_rs.sem, l_rs.up())

        def l2_dve():
            for m in range(8):
                v, pieces = vec_of(m)
                n = pieces[-1][1]
                dve_.wait_ge(l_rs.sem, m + 1)
                dve_.tensor_tensor(v, v, sqb[m % 2][:, 0:n], ALU.mult).then_inc(l_done.sem, l_done.up())
            dve_.wait_ge(l_done.sem, 8)
            for t in range(NTA):
                for dst_ in (ktok, vtok):
                    bank = tturn.bank(dve_)
                    dve_.tensor_copy(dst_[:, t, :], bank).then_inc(tturn.copied.sem, tturn.copied.up())

        def owed_last(m, j):
            return m == 0 and j == 0

        def l2_pe():
            for m in range(8):
                v, pieces = vec_of(m)
                pe_.wait_ge(l_sq.sem, m + 1)
                if m == 0:
                    pe_.wait_ge(cf_ev.sem, 4)
                    pe_.wait_ge(cf_read.sem, 4)
                if m >= 2:
                    pe_.wait_ge(l_rs.sem, m - 1)
                for j, (a, b) in enumerate(pieces):
                    mm = pe_.matmul(PS[:, (m % 2) * 2 + j, 0:b - a], ones, sqb[m % 2][:, a:b], start=True, stop=True)
                    if owed_last(m, j):
                        mm.then_inc(w_used.sem, w_used.up())
                mm.then_inc(l_mm.sem, l_mm.up())
            pe_.wait_ge(l_done.sem, 4)
            for t in range(NTA):
                for src in (kT, vT):
                    tturn.pe([(src[:, h, t * P:(t + 1) * P], slice(h * P, (h + 1) * P)) for h in range(4)])

        beta, gg = S[:, 160:208], S[:, 208:256]
        gc, dl, egc, ekd = S[:, 256:304], S[:, 304:352], S[:, 352:400], S[:, 400:448]
        GLS = sb("chunk_decay", 2 * NTA * 8)
        gs_e, gs_in, gs_ready, gc_mm, gc_ev, gx, gx_done = (sig(n) for n in ("gs_e", "gs_in", "gs_ready", "gc_mm", "gc_ev", "gx", "gx_done"))
        ba5 = S[:, 64:160].rearrange("p (t d c h) -> p t d c h", t=NTA, d=2, c=2)
        tmp8 = SQ[:, 0:48]
        tmp9 = SQ[:, 48:96]

        def g4(a):
            return a.rearrange("p (t d h) -> p t d h", t=NTA, d=2)

        def gates_dve():
            dve_.wait_ge(ba_ev.sem, 1)
            dve_.wait_ge(ld_bc.sem, 16 * N_BC)
            for d in range(2):
                dve_.tensor_copy(g4(beta)[:, :, d, :], ba5[:, :, d, 0, :]).then_inc(own_v.sem, own_v.up())
                dve_.wait_ge(own_v.sem, own_v.n)
                b = dtb[:, d * 4:d * 4 + 4].rearrange("p (o h) -> p o h", o=1).to_broadcast([P, NTA, 4])
                dve_.tensor_tensor(g4(gg)[:, :, d, :], ba5[:, :, d, 1, :], b, ALU.add).then_inc(own_v.sem, own_v.up())
                dve_.wait_ge(own_v.sem, own_v.n)
            dve_.tensor_scalar(tmp8, gg, -1.0, None, ALU.mult).then_inc(gs_in.sem, gs_in.up())
            dve_.wait_ge(gs_in.sem, 1)
            dve_.tensor_tensor(tmp8, tmp8, gg, ALU.min).then_inc(gs_in.sem, gs_in.up())
            dve_.wait_ge(gs_e.sem, 4)
            dve_.tensor_scalar(beta, beta, 1.0, None, ALU.add).then_inc(own_v.sem, own_v.up())
            dve_.wait_ge(own_v.sem, own_v.n)
            dve_.reciprocal(beta, beta).then_inc(own_v.sem, own_v.up())
            dve_.wait_ge(own_v.sem, own_v.n)
            dve_.tensor_scalar(gg, gg, 0.0, None, ALU.max).then_inc(own_v.sem, own_v.up())
            dve_.wait_ge(own_v.sem, own_v.n)
            dve_.tensor_tensor(gg, gg, tmp8, ALU.add).then_inc(own_v.sem, own_v.up())
            dve_.wait_ge(own_v.sem, own_v.n)
            a = alog.rearrange("p (o c) -> p o c", o=1).to_broadcast([P, NTA, 8])
            g3 = gg.rearrange("p (t c) -> p t c", t=NTA)
            dve_.scalar_tensor_tensor(g3, g3, -1.0, a, ALU.mult, ALU.mult).then_inc(gs_ready.sem, gs_ready.up())
            dve_.wait_ge(gc_mm.sem, 1)
            dve_.tensor_copy(gc, PS[:, 0, 0:48]).then_inc(gc_ev.sem, gc_ev.up())
            dve_.tensor_copy(dl, PS[:, 0, 64:112]).then_inc(own_v.sem, own_v.up())
            dve_.wait_ge(own_v.sem, own_v.n)
            dve_.wait_ge(gc_ev.sem, 1)
            dve_.tensor_tensor(dl, dl, gc, ALU.subtract).then_inc(gx.sem, gx.up())
            dve_.tensor_copy(GLS[:, :], PS[:, 0, 128:224]).then_inc(gx.sem, gx.up())
            dve_.wait_ge(gx_done.sem, 3)
            dve_.tensor_tensor(ekd, ekd, beta, ALU.mult).then_inc(own_v.sem, own_v.up())
            dve_.wait_ge(own_v.sem, own_v.n)

        def gates_act():
            act_.wait_ge(gs_in.sem, 2)
            act_.activation(beta, beta, ACT.Exp, scale=-1.0).then_inc(gs_e.sem, gs_e.up())
            act_.activation(tmp8, tmp8, ACT.Exp).then_inc(gs_e.sem, gs_e.up())
            act_.wait_ge(gs_e.sem, gs_e.n)
            act_.activation(tmp8, tmp8, ACT.Ln, bias=1.0).then_inc(gs_e.sem, gs_e.up())
            act_.activation(alog, alog, ACT.Exp).then_inc(gs_e.sem, gs_e.up())
            act_.wait_ge(gx.sem, 2)
            act_.activation(egc, gc, ACT.Exp).then_inc(gx_done.sem, gx_done.up())
            act_.activation(ekd, dl, ACT.Exp).then_inc(gx_done.sem, gx_done.up())
            act_.activation(GLS[:, :], GLS[:, :], ACT.Exp).then_inc(gx_done.sem, gx_done.up())

        def gates_pe():
            pe_.wait_ge(gs_ready.sem, 1)
            pe_.wait_ge(l_rs.sem, 8)
            g3 = gg.rearrange("p (t c) -> p t c", t=NTA)
            for t in range(NTA):
                for d in range(2):
                    o = t * 8 + d * 4
                    pe_.matmul(PS[:, 0, o:o + 4], tri[d], g3[:, t, d * 4:d * 4 + 4], start=True, stop=True)
            for t in range(NTA):
                pe_.matmul(PS[:, 0, 64 + t * 8:72 + t * 8], blk, g3[:, t, :], start=True, stop=True)
            for t in range(NTA):
                for o in range(2):
                    n = 128 + (2 * t + o) * 8
                    mm = pe_.matmul(PS[:, 0, n:n + 8], half_of[o], g3[:, t, :], start=True, stop=True)
            mm.then_inc(gc_mm.sem, gc_mm.up())

        names = ("dt", "lt", "m", "mt", "t1", "intra", "qd", "kd", "u", "wt", "kg")
        bufs = [{n: AR[:, (s * len(names) + j) * 512:(s * len(names) + j + 1) * 512] for j, n in enumerate(names)} for s in range(2)]
        state = [ST[:, d * 512:(d + 1) * 512] for d in range(2)]
        tile_at = [[0, 1, 2, 3, 4, 5], [1, 0, 5, 4, 3, 2]]
        r_mm, g_mm, q_mm, r_relu, r_exp, dt_r, lt_r, intra_r, qd_r, kd_r, kg_r = ([sig(f"{n}{d}") for d in range(2)] for n in
            ("r_mm", "g_mm", "q_mm", "r_relu", "r_exp", "dt_r", "lt_r", "intra_r", "qd_r", "kd_r", "kg_r"))
        tp_mm, m_ev, t1_mm, t1_ev, mt_mm, mt_ev, uw_mm, u_ev, w_ev = ([sig(f"{n}{d}") for d in range(2)] for n in
            ("tp_mm", "m_ev", "t1_mm", "t1_ev", "mt_mm", "mt_ev", "uw_mm", "u_ev", "w_ev"))
        ws_mm, vn_r, o_mm, o_ev, ds_mm, s_ev = ([sig(f"{n}{d}") for d in range(2)] for n in
            ("ws_mm", "vn_r", "o_mm", "o_ev", "ds_mm", "s_ev"))
        s_zero = sig("s_zero")

        def bank(d, n):
            return PS[:, 3 * d + n, :]

        def hh(h):
            return slice(h * P, (h + 1) * P)

        def scal(a, t, d, h):
            n = t * 8 + d * 4 + h
            return a[:, n:n + 1]

        def order_of(d):
            return (0, 1) if d == 0 else (1, 0)

        def delta_pe():
            pe_.wait_ge(gx_done.sem, 3)
            pe_.wait_ge(tturn.copied.sem, 2 * NTA)
            pe_.wait_ge(cfturn.copied.sem, NT)
            for s in range(NTA):
                for d in range(2):
                    t = tile_at[d][s]
                    if s >= 1:
                        pe_.wait_ge(s_ev[d].sem, 2 * s)
                        if o_mm[d].n:
                            pe_.wait_ge(o_ev[d].sem, o_mm[d].n)
                    for h in range(4):
                        mm = pe_.matmul(bank(d, 0)[:, hh(h)], scal(gg, t, d, h).to_broadcast([P, P]), tri[d], start=True, stop=True)
                    mm.then_inc(r_mm[d].sem, r_mm[d].up())
                    for h in range(4):
                        kk = kT[:, h, t * P:(t + 1) * P]
                        mm = pe_.matmul(bank(d, 1)[:, hh(h)], kk, kk, start=True, stop=True)
                    mm.then_inc(g_mm[d].sem, g_mm[d].up())
                    if t >= NCT:
                        for h in range(4):
                            mm = pe_.matmul(bank(d, 2)[:, hh(h)], kT[:, h, t * P:(t + 1) * P], qT[:, h, (t - NCT) * P:(t - NCT + 1) * P],
                                            start=True, stop=True)
                        mm.then_inc(q_mm[d].sem, q_mm[d].up())
                for d in range(2):
                    pe_.wait_ge(mt_ev[d].sem, INV * s + 1)
                    if tile_at[d][s] >= NCT:
                        pe_.wait_ge(intra_r[d].sem, s - 1)
                    turn_m(d)
                for l in range(1, INV):
                    for d in range(2):
                        b = bufs[d]
                        pe_.wait_ge(m_ev[d].sem, (INV - 1) * s + l)
                        pe_.wait_ge(mt_ev[d].sem, INV * s + l)
                        for h in range(4):
                            mm = pe_.matmul(bank(d, 0)[:, hh(h)], b["lt"][:, hh(h)], b["m"][:, hh(h)], start=True, stop=True)
                        mm.then_inc(t1_mm[d].sem, t1_mm[d].up())
                    for d in range(2):
                        b = bufs[d]
                        pe_.wait_ge(t1_ev[d].sem, (INV - 1) * s + l)
                        for h in range(4):
                            mm = pe_.matmul(bank(d, 1)[:, hh(h)], b["t1"][:, hh(h)], b["mt"][:, hh(h)], start=True, stop=True)
                        mm.then_inc(mt_mm[d].sem, mt_mm[d].up())
                    if l in LATER_LEVELS:
                        later.pe()
                    if l < INV - 1:
                        for d in range(2):
                            pe_.wait_ge(mt_ev[d].sem, INV * s + l + 1)
                            turn_m(d)
                for d in range(2):
                    b, t = bufs[d], tile_at[d][s]
                    pe_.wait_ge(mt_ev[d].sem, INV * (s + 1))
                    pe_.wait_ge(kg_r[d].sem, s + 1)
                    for h in range(4):
                        mm = pe_.matmul(bank(d, 0)[:, hh(h)], b["mt"][:, hh(h)], vtok[:, t, hh(h)], start=True, stop=True)
                    for h in range(4):
                        mm = pe_.matmul(bank(d, 2)[:, hh(h)], b["kg"][:, hh(h)], b["mt"][:, hh(h)], start=True, stop=True)
                    mm.then_inc(uw_mm[d].sem, uw_mm[d].up())
                for n in range(2):
                    for d in range(2):
                        b = bufs[d]
                        pe_.wait_ge(w_ev[d].sem, s + 1)
                        pe_.wait_ge(u_ev[d].sem, s + 1)
                        if s == 0 and n == 0:
                            pe_.wait_ge(s_zero.sem, 2)
                        else:
                            pe_.wait_ge(s_ev[d].sem, 2 * s + n)
                        for h in range(4):
                            mm = pe_.matmul(bank(d, 0)[:, hh(h)], b["wt"][:, hh(h)], state[d][:, hh(h)], start=True, stop=True)
                        mm.then_inc(ws_mm[d].sem, ws_mm[d].up())
                    for d in range(2):
                        b, t = bufs[d], tile_at[d][s]
                        o = order_of(d)[n] * 64
                        pe_.wait_ge(vn_r[d].sem, 2 * s + n + 1)
                        pe_.wait_ge(kd_r[d].sem, s + 1)
                        for h in range(4):
                            mm = pe_.matmul(bank(d, 1)[:, hh(h)], b["kd"][o:o + 64, hh(h)], b["u"][o:o + 64, hh(h)], start=True, stop=True)
                        mm.then_inc(ds_mm[d].sem, ds_mm[d].up())
                        if t >= NCT:
                            if n == 0:
                                pe_.wait_ge(qd_r[d].sem, s - 1)
                            if o_mm[d].n:
                                pe_.wait_ge(o_ev[d].sem, o_mm[d].n)
                            for h in range(4):
                                pe_.matmul(bank(d, 2)[:, hh(h)], b["qd"][:, hh(h)], state[d][:, hh(h)], start=True, stop=False)
                                mm = pe_.matmul(bank(d, 2)[:, hh(h)], b["intra"][:, hh(h)], b["u"][:, hh(h)], start=False, stop=True)
                            mm.then_inc(o_mm[d].sem, o_mm[d].up())

        def turn_m(d):
            b = bufs[d]
            for h in range(4):
                mm = pe_.transpose(bank(d, 2)[:, hh(h)], b["mt"][:, hh(h)], ident)
            mm.then_inc(tp_mm[d].sem, tp_mm[d].up())

        def delta_act():
            for s in range(NTA):
                for d in range(2):
                    b, t = bufs[d], tile_at[d][s]
                    act_.wait_ge(r_mm[d].sem, s + 1)
                    for h in range(4):
                        act_.activation(b["dt"][:, hh(h)], bank(d, 0)[:, hh(h)], ACT.Relu, scale=-1.0, bias=scal(gc, t, d, h)).then_inc(r_relu[d].sem, r_relu[d].up())
                    if t >= NCT:
                        act_.activation(b["qd"], bank(d, 0), ACT.Exp).then_inc(r_exp[d].sem, r_exp[d].up())
                    act_.wait_ge(r_relu[d].sem, 4 * (s + 1))
                    act_.activation(b["dt"], b["dt"], ACT.Exp, scale=-1.0).then_inc(dt_r[d].sem, dt_r[d].up())
                    for h in range(4):
                        ins = act_.activation(b["kg"][:, hh(h)], ktok[:, t, hh(h)], ACT.Copy, scale=scal(egc, t, d, h))
                    ins.then_inc(kg_r[d].sem, kg_r[d].up())
                    for h in range(4):
                        ins = act_.activation(b["kd"][:, hh(h)], ktok[:, t, hh(h)], ACT.Copy, scale=scal(ekd, t, d, h))
                    ins.then_inc(kd_r[d].sem, kd_r[d].up())
                for l in range(INV - 1):
                    for d in range(2):
                        b = bufs[d]
                        act_.wait_ge(tp_mm[d].sem, (INV - 1) * s + l + 1)
                        act_.activation(b["m"], bank(d, 2), ACT.Copy).then_inc(m_ev[d].sem, m_ev[d].up())
                    if l + 1 in LATER_LEVELS:
                        later.act()
                for d in range(2):
                    act_.wait_ge(uw_mm[d].sem, s + 1)
                    act_.activation(bufs[d]["u"], bank(d, 0), ACT.Copy).then_inc(u_ev[d].sem, u_ev[d].up())
                    act_.activation(bufs[d]["wt"], bank(d, 2), ACT.Copy).then_inc(w_ev[d].sem, w_ev[d].up())

        visited = set()

        def delta_dve():
            for d in range(2):
                dve_.memset(state[d], 0.0).then_inc(s_zero.sem, s_zero.up())
            for s in range(NTA):
                for d in range(2):
                    b, t = bufs[d], tile_at[d][s]
                    dve_.wait_ge(dt_r[d].sem, s + 1)
                    for h in range(4):
                        ins = dve_.scalar_tensor_tensor(b["dt"][:, hh(h)], b["dt"][:, hh(h)], scal(beta, t, d, h), tri[d], ALU.mult, ALU.mult)
                        ins.then_inc(own_v.sem, own_v.up())
                    dve_.wait_ge(own_v.sem, own_v.n)
                    dve_.wait_ge(g_mm[d].sem, s + 1)
                    dve_.tensor_tensor(b["lt"], b["dt"], bank(d, 1), ALU.mult).then_inc(own_v.sem, own_v.up())
                    dve_.wait_ge(own_v.sem, own_v.n)
                    up = part(K, (AK_UP if d == 0 else AK_LOW), P)
                    dve_.tensor_tensor(heads4(b["mt"]), heads4(b["lt"]), rep(up), ALU.mult).then_inc(own_v.sem, own_v.up())
                    dve_.wait_ge(own_v.sem, own_v.n)
                    dve_.tensor_tensor(heads4(b["mt"]), rep(ident), heads4(b["mt"]), ALU.subtract).then_inc(mt_ev[d].sem, mt_ev[d].up())
                    if t >= NCT:
                        dve_.wait_ge(q_mm[d].sem, s - 1)
                        dve_.tensor_tensor(b["intra"], b["dt"], bank(d, 2), ALU.mult).then_inc(intra_r[d].sem, intra_r[d].up())
                        dve_.wait_ge(r_exp[d].sem, s - 1)
                        q = qT[:, :, (t - NCT) * P:(t - NCT + 1) * P]
                        dve_.tensor_tensor(heads4(b["qd"]), heads4(b["qd"]), q, ALU.mult).then_inc(qd_r[d].sem, qd_r[d].up())
                for l in range(1, INV):
                    for d in range(2):
                        b = bufs[d]
                        low = part(K, (AK_LOW if d == 0 else AK_UP) + l * P, P)
                        dve_.wait_ge(t1_mm[d].sem, (INV - 1) * s + l)
                        dve_.tensor_tensor(heads4(b["t1"]), heads4(bank(d, 0)), rep(low), ALU.mult).then_inc(t1_ev[d].sem, t1_ev[d].up())
                    for d in range(2):
                        b = bufs[d]
                        dve_.wait_ge(mt_mm[d].sem, (INV - 1) * s + l)
                        dve_.wait_ge(mt_ev[d].sem, INV * s + l)
                        dve_.tensor_tensor(b["mt"], b["mt"], bank(d, 1), ALU.subtract).then_inc(mt_ev[d].sem, mt_ev[d].up())
                for n in range(2):
                    for d in range(2):
                        b = bufs[d]
                        o = order_of(d)[n] * 64
                        dve_.wait_ge(ws_mm[d].sem, 2 * s + n + 1)
                        dve_.tensor_tensor(b["u"][o:o + 64, :], b["u"][o:o + 64, :], bank(d, 0)[o:o + 64, :], ALU.subtract).then_inc(vn_r[d].sem, vn_r[d].up())
                    for d in range(2):
                        b, t = bufs[d], tile_at[d][s]
                        half = order_of(d)[n]
                        o = half * 64
                        dve_.wait_ge(ds_mm[d].sem, 2 * s + n + 1)
                        g = 8 * (2 * t + half) + 4 * d
                        gl = GLS[:, g:g + 4].rearrange("p (h w) -> p h w", w=1).to_broadcast([P, 4, P])
                        if t >= NCT:
                            dve_.wait_ge(o_mm[d].sem, 2 * (s - NCT) + n + 1)
                        if n or s:
                            dve_.wait_ge(s_ev[d].sem, 2 * s + n)
                        else:
                            dve_.wait_ge(s_zero.sem, 2)
                        dve_.tensor_tensor(heads4(state[d]), heads4(state[d]), gl, ALU.mult).then_inc(own_v.sem, own_v.up())
                        dve_.wait_ge(own_v.sem, own_v.n)
                        dve_.tensor_tensor(state[d], state[d], bank(d, 1), ALU.add).then_inc(s_ev[d].sem, s_ev[d].up())
                        if t >= NCT:
                            x = o3[o:o + 64, t - NCT, :]
                            if (t, half) in visited:
                                dve_.wait_ge(o_ev[1 - d].sem, o_ev[1 - d].n)
                                dve_.tensor_tensor(x, x, bank(d, 2)[o:o + 64, :], ALU.add).then_inc(o_ev[d].sem, o_ev[d].up())
                            else:
                                visited.add((t, half))
                                dve_.tensor_copy(x, bank(d, 2)[o:o + 64, :]).then_inc(o_ev[d].sem, o_ev[d].up())

        cfturn = Turn(nc, ctx, "cfturn_a", [PS[:, b, :] for b in (2, 3)], ident)
        cf_sum, cf_sq, cf_rs, cf_silu, cf_n = sig("cf_sum"), sig("cf_sq"), sig("cf_rs"), sig("cf_silu"), sig("cf_n")
        mu, vr = S[:, 448:452], S[:, 452:456]

        def cfturn_pe():
            pe_.wait_ge(cf_conv.sem, 4)
            for t in range(NT):
                cfturn.pe([(cc[:, cch, t * P:(t + 1) * P], slice(cch * P, (cch + 1) * P)) for cch in range(4)])

        def cf_act():
            for t in range(NT):
                b = cfturn.bank(act_)
                act_.activation(cft[:, t, :], b, ACT.Copy, accum_out=mu[:, t:t + 1]).then_inc(cfturn.copied.sem, cfturn.copied.up())
            act_.wait_ge(cf_sum.sem, 1)
            for t in range(NT):
                act_.activation(SQ[:, 0:512] if t % 2 == 0 else SQ[:, 512:1024], cft[:, t, :], ACT.Square, bias=mu[:, t:t + 1], accum_out=vr[:, t:t + 1]).then_inc(cf_sq.sem, cf_sq.up())
                if t:
                    act_.wait_ge(cf_sq.sem, t)
            act_.wait_ge(cf_sq.sem, NT)
            act_.activation(vr, vr, ACT.Ln, scale=1.0 / 512, bias=EPS).then_inc(own_a.sem, own_a.up())
            act_.wait_ge(own_a.sem, own_a.n)
            act_.activation(vr, vr, ACT.Exp, scale=-0.5).then_inc(cf_rs.sem, cf_rs.up())

        def cf_silu_act():
            for t in range(NT):
                act_.wait_ge(cf_n.sem, t + 1)
                act_.activation(cft[:, t, :], cft[:, t, :], ACT.Silu).then_inc(cf_silu.sem, cf_silu.up())

        def cfnorm_dve():
            dve_.wait_ge(cfturn.copied.sem, NT)
            dve_.tensor_scalar(mu, mu, -1.0 / 512, None, ALU.mult).then_inc(cf_sum.sem, cf_sum.up())
            dve_.wait_ge(cf_rs.sem, 1)
            for t in range(NT):
                y = cft[:, t, :]
                dve_.tensor_scalar(y, y, mu[:, t:t + 1], vr[:, t:t + 1], ALU.add, ALU.mult).then_inc(own_v.sem, own_v.up())
                dve_.wait_ge(own_v.sem, own_v.n)
                dve_.tensor_tensor(y, y, LG[:, :], ALU.mult).then_inc(own_v.sem, own_v.up())
                dve_.wait_ge(own_v.sem, own_v.n)
                dve_.tensor_tensor(y, y, LB[:, :], ALU.add).then_inc(cf_n.sem, cf_n.up())

        on_sq, on_rs, z_silu, on_r = sig("on_sq"), sig("on_rs"), sig("z_silu"), sig("on_r")
        osum = S[:, 456:472]
        hturn = Turn(nc, ctx, "hturn_a", [PS[:, b, :] for b in (6, 7)], ident)
        heT = part(AR, 0, KD * T, a=KD)
        w_mm, w_fin = sig("w_mm"), sig("w_fin")

        def zsilu_act():
            for t in range(NT):
                act_.activation(z3[:, t, :], z3[:, t, :], ACT.Silu).then_inc(z_silu.sem, z_silu.up())

        def heads_dve():
            dve_.wait_ge(later.reduced.sem, later.tiles)
            dve_.wait_ge(o_ev[0].sem, 8)
            dve_.wait_ge(o_ev[1].sem, 8)
            for t in range(NT):
                q = SQ[:, (t % 2) * 512:(t % 2) * 512 + 512]
                dve_.tensor_tensor(q, o3[:, t, :], o3[:, t, :], ALU.mult).then_inc(own_v.sem, own_v.up())
                dve_.wait_ge(own_v.sem, own_v.n)
                dve_.tensor_reduce(osum[:, 4 * t:4 * t + 4], heads4(q), AX.X, ALU.add).then_inc(on_sq.sem, on_sq.up())
            dve_.wait_ge(on_rs.sem, 1)
            dve_.wait_ge(z_silu.sem, NT)
            for t in range(NT):
                o = o3[:, t, :]
                r = osum[:, 4 * t:4 * t + 4].rearrange("p (h w) -> p h w", w=1).to_broadcast([P, 4, P])
                dve_.tensor_tensor(heads4(o), heads4(o), r, ALU.mult).then_inc(own_v.sem, own_v.up())
                dve_.wait_ge(own_v.sem, own_v.n)
                dve_.tensor_tensor(heads4(o), heads4(o), rep(NG[:, :]), ALU.mult).then_inc(own_v.sem, own_v.up())
                dve_.wait_ge(own_v.sem, own_v.n)
                dve_.tensor_tensor(o, o, z3[:, t, :], ALU.mult).then_inc(on_r.sem, on_r.up())
            for t in range(NT):
                for half in range(2):
                    c_ = slice(half * 512, (half + 1) * 512)
                    n = 2 * t + half
                    dve_.wait_ge(w_mm.sem, n + 1)
                    tmp = SQ[:, half * 512:(half + 1) * 512]
                    dve_.tensor_tensor(tmp, PS[:, n % 4, :], GB[:, c_], ALU.mult).then_inc(own_v.sem, own_v.up())
                    dve_.wait_ge(own_v.sem, own_v.n)
                    dve_.tensor_tensor(x3[:, t, c_], x3[:, t, c_], tmp, ALU.add).then_inc(w_fin.sem, w_fin.up())

        def heads_act():
            act_.wait_ge(on_sq.sem, NT)
            act_.activation(osum, osum, ACT.Ln, scale=1.0 / P, bias=EPS).then_inc(own_a.sem, own_a.up())
            act_.wait_ge(own_a.sem, own_a.n)
            act_.activation(osum, osum, ACT.Exp, scale=-0.5).then_inc(on_rs.sem, on_rs.up())
            for k in range(KD):
                b = hturn.bank(act_)
                act_.activation(heT[:, k, :], b, ACT.Copy).then_inc(hturn.copied.sem, hturn.copied.up())

        def heads_pe():
            pe_.wait_ge(cf_silu.sem, NT)
            pe_.wait_ge(s_ev[0].sem, 12)
            pe_.wait_ge(s_ev[1].sem, 12)
            for k in list(range(4, 8)) + list(range(4)):
                if k == 0:
                    pe_.wait_ge(on_r.sem, NT)
                src = o3 if k < 4 else cft
                hturn.pe([(src[:, t, (k % 4) * P:(k % 4 + 1) * P], slice(t * P, (t + 1) * P)) for t in range(NT)])
            pe_.wait_ge(hturn.copied.sem, KD)
            w = [take(), None]
            pe_.wait_ge(w_loaded[slot_of[taken[0]]].sem, 16 * loads_of(taken[0]))
            w[1] = slot(taken[0])
            for t in range(NT):
                for half in range(2):
                    n = 2 * t + half
                    if n >= 4:
                        pe_.wait_ge(w_fin.sem, n - 3)
                    for k in range(KD):
                        mm = product(PS[:, n % 4, :], heT[:, (k + 4) % 8, t * P:(t + 1) * P], w[k // 4][:, k % 4, half * 512:(half + 1) * 512],
                                     start=k == 0, stop=k == KD - 1)
                    mm.then_inc(w_mm.sem, w_mm.up())

        block = ctx.enter_context(nc.Block())

        @block.sync
        def _(sp):
            loads_sp(sp)
            for n in range(len(tiles)):
                if n == len(tiles) - 2:
                    sp.wait_ge(later.scaled.sem, 2 * later.tiles)
                if before[n] is not None:
                    sp.wait_ge(w_used.sem, before[n] + 1)
                sp.dma_start(slot(n), tiles[n]).then_inc(w_loaded[slot_of[n]].sem, w_loaded[slot_of[n]].up(16))
            for t in range(NT):
                sp.wait_ge(w_fin.sem, 2 * (t + 1))
                sp.dma_start(x_out[t * P:(t + 1) * P, :], x3[:, t, :]).then_inc(stored.sem, stored.up(16))
            sp.wait_ge(stored.sem, 16 * NT)

        @block.gpsimd
        def _(pool):
            pool.wait_ge(silu.sem, 2)
            pool.wait_ge(w_used.sem, 13)
            pool.wait_ge(cf_sq.sem, NT)
            later.pool()

        @block.tensor
        def _(pe):
            cond_pe()
            mod_pe()
            pe.wait_ge(gb_ready.sem, 1)
            norm_pe()
            proj_pe()
            rest_pe()
            l2_pe()
            gates_pe()
            cfturn_pe()
            delta_pe()
            heads_pe()

        @block.scalar
        def _(act):
            loads_act(act)
            cond_act()
            square_act()
            mod_act()
            norm_act()
            proj_act()
            rest_act()
            l2_act()
            gates_act()
            cf_act()
            zsilu_act()
            cf_silu_act()
            delta_act()
            heads_act()
            later.wait_stored(act)

        @block.vector
        def _(dve):
            cond_dve()
            norm_dve()
            mod_dve()
            turned_dve()
            proj_dve()
            cf_dve()
            l2_dve()
            gates_dve()
            cfnorm_dve()
            delta_dve()
            heads_dve()


NE, GROUPS, KEEP, TOP6 = 64, 8, 4, 6
DE = 256
ROUTED = 2.5
NBLK = NE + T * TOP6 // P
UNROLL = 3
NBLK_PAD = -(-NBLK // UNROLL) * UNROLL
BK_ID, BK_STRICT, BK_ONES, BK_TOK, BK_EXP, BK_LOWER, BK_OVER = 0, P, 2 * P, 3 * P, 3 * P + 4, 3 * P + 4 + NE, 3 * P + 4 + NE + NE
BK_COLS = BK_OVER + NBLK_PAD


def moe_constants():
    c = np.zeros((P, BK_COLS), np.float32)
    i = np.arange(P)
    c[:, BK_ID:BK_ID + P] = np.eye(P)
    c[:, BK_STRICT:BK_STRICT + P] = i[:, None] < i[None]
    c[:, BK_ONES:BK_ONES + P] = 1.0
    c[:, BK_TOK:BK_TOK + NT] = i[:, None] + P * np.arange(NT)[None]
    c[:, BK_EXP:BK_EXP + NE] = np.arange(NE)[None]
    g = np.arange(GROUPS)
    c[:, BK_LOWER:BK_LOWER + NE] = (g[None, :] < g[:, None]).reshape(-1)[None]
    c[:, BK_OVER:BK_OVER + NBLK_PAD] = np.arange(NBLK_PAD)[None]
    return c


def moe(nc, x_in, x_out, mod, b_mod, g_ffn, router_w, router_bias, w_gate, w_up, w_down, s_gate, s_up, s_down,
        g_final, consts):
    pe_, act_, dve_, pool_ = nc.tensor, nc.scalar, nc.vector, nc.gpsimd
    h_rows = nc.dram_tensor("h_rows", [T, D], F32).ap()
    slot_tok = nc.dram_tensor("slot_tok", [P * NBLK_PAD, 1], I32).ap()
    y_rows = nc.dram_tensor("y_rows", [NBLK_PAD * P, D], F32).ap()
    with Scope(nc) as ctx:
        def sb(name, cols, parts=P, dt=F32):
            return ctx.enter_context(nc.sbuf_tensor(f"{name}_m", [parts, cols], dt))

        def sig(name):
            return Signal(ctx, nc, f"{name}_m")

        X = sb("x", NT * D)
        HT = sb("hT", KD * T)
        SH = sb("shared", NT * D)
        XN = sb("xn", NT * D)
        W = sb("w", UNROLL * 6144)
        GA = sb("gathered", UNROLL * D)
        GT = sb("gatheredT", 2 * D)
        YB = sb("yblock", UNROLL * D)
        K = sb("consts", BK_COLS)
        VR, VC, MC = sb("vrows", P), sb("vcols", 64), sb("modcols", 16)
        S = sb("small", 64)
        SA, AT = sb("silu", 2 * DE), sb("aT", 2 * DE)
        RW = sb("router", KD * NE)
        RB = sb("rbias", NE)
        R = [sb(f"route{i}", NT * NE) for i in range(7)]
        R4 = sb("eights", NT * 64)
        SL = sb("slots", NT * 8)
        WK = sb("slotw", NT * 8)
        SLI, ADR = sb("sloti", NT * 8, dt=I32), sb("addr", NT * 8, dt=I32)
        TOKI = sb("toki", NT, dt=I32)
        TAB = sb("table", NBLK_PAD, dt=I32)
        IDX = sb("index", UNROLL, dt=I32)
        CI = sb("counts", 4 + NBLK_PAD, dt=I32)
        CF = sb("countsf", 4 * NE + NBLK_PAD + NE)
        GB = sb("gateb", D)
        GF = sb("gfinal", D)
        PS = ctx.enter_context(nc.psum_tensor("ps_m", [P, 8, 512], F32))

        x3 = X[:, :].rearrange("p (t d) -> p t d", t=NT)
        sh3 = SH[:, :].rearrange("p (t d) -> p t d", t=NT)
        xn = XN[:, :].rearrange("p (t d) -> p t d", t=NT)
        hT = HT[:, :].rearrange("p (k t) -> p k t", k=KD)
        rw = RW[:, :].rearrange("p (k e) -> p k e", k=KD)
        ident, strict, ones = K[:, BK_ID:BK_ID + P], K[:, BK_STRICT:BK_STRICT + P], K[:, BK_ONES:BK_ONES + P]
        ms, rs = S[:, 0:8], S[:, 8:12]
        own_v, own_a = sig("dve"), sig("act")
        gu_w = [W[:, r * 6144:r * 6144 + 4096].rearrange("p (k m n) -> p k m n", k=KD, m=2) for r in range(UNROLL)]
        dn_w = [W[:, r * 6144 + 4096:(r + 1) * 6144].rearrange("p (k n) -> p k n", k=2) for r in range(UNROLL)]

        ld_const, ld_vec, ld_x, ld_row, ld_rw, ld_sh = (sig(n) for n in ("ld_const", "ld_vec", "ld_x", "ld_row", "ld_rw", "ld_sh"))
        w_loaded = [sig(f"w_loaded{r}") for r in range(UNROLL)]
        w_used = [sig(f"w_used{r}") for r in range(UNROLL)]
        stored = sig("stored")

        vec_turned, vec_cols, mod_cols, gb_ready = sig("vec_turned"), sig("vec_cols"), sig("mod_cols"), sig("gb_ready")

        def vec_pe():
            pe_.wait_ge(ld_const.sem, 16)
            pe_.wait_ge(ld_vec.sem, 16 * 3)
            pe_.transpose(PS[:, 0, 0:40], VR[0:40, :], ident[0:40, 0:40]).then_inc(vec_turned.sem, vec_turned.up())

        def mod_dve():
            dve_.wait_ge(vec_turned.sem, 1)
            dve_.tensor_copy(VC[:, 0:40], PS[:, 0, 0:40]).then_inc(vec_cols.sem, vec_cols.up())
            dve_.wait_ge(vec_cols.sem, 1)
            dve_.tensor_tensor(MC[:, :], VC[:, 24:40], VC[:, 0:16], ALU.add).then_inc(own_v.sem, own_v.up())
            dve_.wait_ge(own_v.sem, own_v.n)
            dve_.scalar_tensor_tensor(MC[:, 8:16], MC[:, 8:16], 1.0, VC[:, 16:24], ALU.add, ALU.mult).then_inc(mod_cols.sem, mod_cols.up())

        def gate_dve():
            dve_.wait_ge(ld_row.sem, 16 * 3)
            dve_.tensor_tensor(GB[:, :], GB[:, :], GA[:, 0:D], ALU.add).then_inc(gb_ready.sem, gb_ready.up())

        sq, rs_s, xn_s, fin_sq, fin_rs = sig("sq"), sig("rs"), sig("xn"), sig("fin_sq"), sig("fin_rs")
        nturn = Turn(nc, ctx, "norm_m", [PS[:, b, :] for b in (6, 7)], ident)
        rturn = Turn(nc, ctx, "rows_m", [PS[:, b, :] for b in (6, 7)], ident)
        rows_stored = sig("rows_stored")

        def norm_act():
            act_.wait_ge(ld_x.sem, 16)
            for t in range(NT):
                act_.activation(HT[:, t * D:(t + 1) * D], x3[:, t, :], ACT.Square, accum_out=ms[:, t:t + 1]).then_inc(sq.sem, sq.up())
            act_.wait_ge(sq.sem, NT)
            act_.activation(rs, ms[:, 0:NT], ACT.Ln, scale=1.0 / D, bias=EPS).then_inc(own_a.sem, own_a.up())
            act_.wait_ge(own_a.sem, own_a.n)
            act_.activation(rs, rs, ACT.Exp, scale=-0.5).then_inc(rs_s.sem, rs_s.up())

        def norm_dve():
            dve_.wait_ge(rs_s.sem, 1)
            for t in range(NT):
                dve_.tensor_scalar(xn[:, t, :], x3[:, t, :], rs[:, t:t + 1], None, ALU.mult).then_inc(xn_s.sem, xn_s.up())
            dve_.wait_ge(mod_cols.sem, 1)
            for k in range(KD):
                bank = nturn.bank(dve_)
                dve_.tensor_scalar(hT[:, k, :], bank, MC[:, 8 + k:9 + k], MC[:, k:k + 1], ALU.mult, ALU.add).then_inc(nturn.copied.sem, nturn.copied.up())
            for n in range(2 * NT):
                bank = rturn.bank(dve_)
                dve_.tensor_copy(XN[:, n * 512:(n + 1) * 512], bank).then_inc(rturn.copied.sem, rturn.copied.up())

        def norm_pe():
            pe_.wait_ge(xn_s.sem, NT)
            for k in range(KD):
                nturn.pe([(xn[:, t, k * P:(k + 1) * P], slice(t * P, (t + 1) * P)) for t in range(NT)])
            pe_.wait_ge(nturn.copied.sem, KD)
            for n in range(2 * NT):
                t, half = n // 2, n % 2
                rturn.pe([(hT[:, 4 * half + j, t * P:(t + 1) * P], slice(j * P, (j + 1) * P)) for j in range(4)])

        ro_mm, ro_e, ro_mask, ro_pos, ro_posc, ro_slots, ro_tab = (sig(n) for n in ("ro_mm", "ro_e", "ro_mask", "ro_pos", "ro_posc", "ro_slots", "ro_tab"))
        scores, sel, keepf, mask, wd, t1, t2 = [r[:, :] for r in R]

        def v3(a, n=NE):
            return a.rearrange("p (t e) -> p t e", e=n)

        def router_pe():
            pe_.wait_ge(ld_rw.sem, 32)
            for t in range(NT):
                for k in range(KD):
                    mm = pe_.matmul(PS[:, 0, t * NE:(t + 1) * NE], hT[:, k, t * P:(t + 1) * P], rw[:, k, :], start=k == 0, stop=k == KD - 1)
            mm.then_inc(ro_mm.sem, ro_mm.up())

        def router_act():
            act_.wait_ge(ro_mm.sem, 1)
            act_.activation(scores, PS[:, 0, 0:NT * NE], ACT.Exp, scale=-1.0).then_inc(ro_e.sem, ro_e.up())

        def router_dve():
            V = dve_

            V.wait_ge(ro_e.sem, 1)
            V.tensor_scalar(scores, scores, 1.0, None, ALU.add).then_inc(own_v.sem, own_v.up())
            V.wait_ge(own_v.sem, own_v.n)
            V.reciprocal(scores, scores).then_inc(own_v.sem, own_v.up())
            V.wait_ge(own_v.sem, own_v.n)
            rb = RB[:, :].rearrange("p (o e) -> p o e", o=1).to_broadcast([P, NT, NE])
            V.tensor_tensor(v3(sel), v3(scores), rb, ALU.add).then_inc(own_v.sem, own_v.up())
            V.wait_ge(own_v.sem, own_v.n)
            for n in range(NT * GROUPS):
                V.max(R4[:, n * 8:n * 8 + 8], sel[:, n * 8:n * 8 + 8]).then_inc(own_v.sem, own_v.up())
            V.wait_ge(own_v.sem, own_v.n)
            top2 = R4[:, :].rearrange("p (n e) -> p n e", e=8)
            gs = SL[:, 0:NT * GROUPS]
            V.tensor_tensor(gs.rearrange("p (n o) -> p n o", o=1), top2[:, :, 0:1], top2[:, :, 1:2], ALU.add).then_inc(own_v.sem, own_v.up())
            V.wait_ge(own_v.sem, own_v.n)
            lower = K[:, BK_LOWER:BK_LOWER + 64].rearrange("p (a b) -> p a b", a=8)
            for t in range(NT):
                g = gs[:, t * 8:(t + 1) * 8]
                a_ = g.rearrange("p (o b) -> p o b", o=1).to_broadcast([P, 8, 8])
                b_ = g.rearrange("p (a o) -> p a o", o=1).to_broadcast([P, 8, 8])
                u, v = t1[:, t * 64:t * 64 + 64].rearrange("p (a b) -> p a b", a=8), t2[:, t * 64:t * 64 + 64].rearrange("p (a b) -> p a b", a=8)
                V.tensor_tensor(u, a_, b_, ALU.is_gt).then_inc(own_v.sem, own_v.up())
                V.tensor_tensor(v, a_, b_, ALU.is_equal).then_inc(own_v.sem, own_v.up())
                V.wait_ge(own_v.sem, own_v.n)
                V.tensor_tensor(v, v, lower, ALU.mult).then_inc(own_v.sem, own_v.up())
                V.wait_ge(own_v.sem, own_v.n)
                V.tensor_tensor(u, u, v, ALU.add).then_inc(own_v.sem, own_v.up())
                V.wait_ge(own_v.sem, own_v.n)
                V.tensor_reduce(WK[:, t * 8:(t + 1) * 8], u, AX.X, ALU.add).then_inc(own_v.sem, own_v.up())
                V.wait_ge(own_v.sem, own_v.n)
            V.tensor_scalar(WK[:, :], WK[:, :], KEEP - 0.5, NEG, ALU.is_gt, ALU.mult).then_inc(own_v.sem, own_v.up())
            V.wait_ge(own_v.sem, own_v.n)
            gk = WK[:, :].rearrange("p (n o) -> p n o", o=1).to_broadcast([P, NT * GROUPS, 8])
            s8 = sel.rearrange("p (n e) -> p n e", e=8)
            V.tensor_tensor(s8, s8, gk, ALU.add).then_inc(own_v.sem, own_v.up())
            V.wait_ge(own_v.sem, own_v.n)
            for t in range(NT):
                V.max(R4[:, t * 8:t * 8 + 8], sel[:, t * NE:(t + 1) * NE]).then_inc(own_v.sem, own_v.up())
            V.wait_ge(own_v.sem, own_v.n)
            sixth = R4[:, 0:NT * 8].rearrange("p (t e) -> p t e", e=8)[:, :, 5:6].to_broadcast([P, NT, NE])
            V.tensor_tensor(v3(mask), v3(sel), sixth, ALU.is_gt).then_inc(own_v.sem, own_v.up())
            V.tensor_tensor(v3(t1), v3(sel), sixth, ALU.is_equal).then_inc(own_v.sem, own_v.up())
            V.wait_ge(own_v.sem, own_v.n)
            above = S[:, 32:36]
            V.tensor_reduce(above, v3(mask), AX.X, ALU.add).then_inc(own_v.sem, own_v.up())
            V.wait_ge(own_v.sem, own_v.n)
            V.tensor_scalar(above, above, -1.0, float(TOP6), ALU.mult, ALU.add).then_inc(own_v.sem, own_v.up())
            V.wait_ge(own_v.sem, own_v.n)
            for t in range(NT):
                V.tensor_tensor_scan(t2[:, t * NE:(t + 1) * NE], ones[:, 0:NE], t1[:, t * NE:(t + 1) * NE], 0.0, ALU.mult, ALU.add).then_inc(own_v.sem, own_v.up())
            V.wait_ge(own_v.sem, own_v.n)
            V.tensor_tensor(v3(t2), v3(t2), above.rearrange("p (t o) -> p t o", o=1).to_broadcast([P, NT, NE]), ALU.is_le).then_inc(own_v.sem, own_v.up())
            V.wait_ge(own_v.sem, own_v.n)
            V.tensor_tensor(t1, t1, t2, ALU.mult).then_inc(own_v.sem, own_v.up())
            V.wait_ge(own_v.sem, own_v.n)
            V.tensor_tensor(mask, mask, t1, ALU.add).then_inc(ro_mask.sem, ro_mask.up())
            V.wait_ge(ro_mask.sem, 1)
            V.tensor_tensor(wd, scores, mask, ALU.mult).then_inc(own_v.sem, own_v.up())
            V.wait_ge(own_v.sem, own_v.n)
            V.tensor_reduce(above, v3(wd), AX.X, ALU.add).then_inc(own_v.sem, own_v.up())
            V.wait_ge(own_v.sem, own_v.n)
            V.reciprocal(above, above).then_inc(own_v.sem, own_v.up())
            V.wait_ge(own_v.sem, own_v.n)
            V.tensor_scalar(above, above, ROUTED, None, ALU.mult).then_inc(own_v.sem, own_v.up())
            V.wait_ge(own_v.sem, own_v.n)
            V.tensor_tensor(v3(wd), v3(wd), above.rearrange("p (t o) -> p t o", o=1).to_broadcast([P, NT, NE]), ALU.mult).then_inc(own_v.sem, own_v.up())
            V.wait_ge(own_v.sem, own_v.n)
            shared_dve()
            V.wait_ge(ro_pos.sem, 1)
            cnt, nob, cum = CF[:, 0:NE], CF[:, NE:2 * NE], CF[:, 2 * NE:3 * NE]
            V.tensor_copy(cnt, PS[:, 0, 0:NE]).then_inc(own_v.sem, own_v.up())
            V.wait_ge(own_v.sem, own_v.n)
            V.tensor_scalar(nob, cnt, float(P), None, ALU.is_gt).then_inc(own_v.sem, own_v.up())
            V.wait_ge(own_v.sem, own_v.n)
            for j in (2, 3):
                V.scalar_tensor_tensor(nob, cnt, float(j * P), nob, ALU.is_gt, ALU.add).then_inc(own_v.sem, own_v.up())
                V.wait_ge(own_v.sem, own_v.n)
            V.tensor_tensor_scan(cum, ones[:, 0:NE], nob, 0.0, ALU.mult, ALU.add).then_inc(own_v.sem, own_v.up())
            V.wait_ge(own_v.sem, own_v.n)
            V.tensor_scalar(CF[:, 3 * NE:3 * NE + 1], cum[:, NE - 1:NE], float(NE + UNROLL - 1), None, ALU.add).then_inc(own_v.sem, own_v.up())
            V.wait_ge(own_v.sem, own_v.n)
            be = CF[:, 4 * NE:4 * NE + NBLK_PAD]
            for b in range(NE, NBLK_PAD):
                tmp = t1[:, (b - NE) % 2 * NE:(b - NE) % 2 * NE + NE]
                V.tensor_scalar(tmp, cum, float(b - NE), 0.0, ALU.is_le, ALU.add, accum_out=be[:, b:b + 1]).then_inc(own_v.sem, own_v.up())
                if b > NE:
                    V.wait_ge(own_v.sem, own_v.n - 1)
            V.tensor_copy(be[:, 0:NE], K[:, BK_EXP:BK_EXP + NE]).then_inc(own_v.sem, own_v.up())
            V.wait_ge(own_v.sem, own_v.n)
            V.tensor_scalar(be, be, float(NE - 1), None, ALU.min).then_inc(own_v.sem, own_v.up())
            V.wait_ge(own_v.sem, own_v.n)
            V.tensor_copy(CI[:, 4:4 + NBLK_PAD], be).then_inc(own_v.sem, own_v.up())
            V.wait_ge(own_v.sem, own_v.n)
            V.tensor_copy(CI[:, 0:1], CF[:, 3 * NE:3 * NE + 1]).then_inc(own_v.sem, own_v.up())
            V.wait_ge(own_v.sem, own_v.n)
            pos = t2
            V.tensor_copy(pos, PS[:, 1, 0:NT * NE]).then_inc(own_v.sem, own_v.up())
            V.wait_ge(own_v.sem, own_v.n)
            j = t1
            V.tensor_scalar(j, pos, float(P), None, ALU.is_ge).then_inc(own_v.sem, own_v.up())
            V.wait_ge(own_v.sem, own_v.n)
            for n in (2, 3):
                V.scalar_tensor_tensor(j, pos, float(n * P), j, ALU.is_ge, ALU.add).then_inc(own_v.sem, own_v.up())
                V.wait_ge(own_v.sem, own_v.n)
            over = CF[:, 4 * NE + NBLK_PAD:5 * NE + NBLK_PAD]
            V.tensor_tensor(over, cum, nob, ALU.subtract).then_inc(own_v.sem, own_v.up())
            V.wait_ge(own_v.sem, own_v.n)
            V.tensor_tensor(over, over, K[:, BK_EXP:BK_EXP + NE], ALU.subtract).then_inc(own_v.sem, own_v.up())
            V.wait_ge(own_v.sem, own_v.n)
            V.tensor_scalar(over, over, float(NE - 1), None, ALU.add).then_inc(own_v.sem, own_v.up())
            V.wait_ge(own_v.sem, own_v.n)
            V.tensor_scalar(sel, j, 0.5, None, ALU.is_gt).then_inc(own_v.sem, own_v.up())
            V.wait_ge(own_v.sem, own_v.n)
            V.tensor_tensor(v3(sel), v3(sel), over.rearrange("p (o e) -> p o e", o=1).to_broadcast([P, NT, NE]), ALU.mult).then_inc(own_v.sem, own_v.up())
            V.wait_ge(own_v.sem, own_v.n)
            eb = K[:, BK_EXP:BK_EXP + NE].rearrange("p (o e) -> p o e", o=1).to_broadcast([P, NT, NE])
            V.tensor_tensor(v3(sel), v3(sel), eb, ALU.add).then_inc(own_v.sem, own_v.up())
            V.wait_ge(own_v.sem, own_v.n)
            V.scalar_tensor_tensor(sel, sel, float(P), pos, ALU.mult, ALU.add).then_inc(own_v.sem, own_v.up())
            V.wait_ge(own_v.sem, own_v.n)
            V.scalar_tensor_tensor(sel, sel, 1.0, mask, ALU.add, ALU.mult).then_inc(own_v.sem, own_v.up())
            V.wait_ge(own_v.sem, own_v.n)
            for t in range(NT):
                V.max(SL[:, t * 8:(t + 1) * 8], sel[:, t * NE:(t + 1) * NE]).then_inc(own_v.sem, own_v.up())
            V.wait_ge(own_v.sem, own_v.n)
            for t in range(NT):
                for k in range(TOP6):
                    n = t * TOP6 + k
                    o = t1[:, n % 2 * NE:n % 2 * NE + NE]
                    if n >= 2:
                        V.wait_ge(own_v.sem, own_v.n - 1)
                    V.scalar_tensor_tensor(o, sel[:, t * NE:(t + 1) * NE], SL[:, t * 8 + k:t * 8 + k + 1], wd[:, t * NE:(t + 1) * NE],
                                           ALU.is_equal, ALU.mult, accum_out=WK[:, t * 8 + k:t * 8 + k + 1]).then_inc(own_v.sem, own_v.up())
            V.wait_ge(own_v.sem, own_v.n)
            V.tensor_scalar(SL[:, :], SL[:, :], 1.0, 0.0, ALU.subtract, ALU.max).then_inc(own_v.sem, own_v.up())
            V.wait_ge(own_v.sem, own_v.n)
            V.tensor_copy(SLI[:, :], SL[:, :]).then_inc(own_v.sem, own_v.up())
            V.wait_ge(own_v.sem, own_v.n)
            V.tensor_scalar(ADR[:, :], SLI[:, :], 7, None, ALU.logical_shift_right).then_inc(own_v.sem, own_v.up())
            V.wait_ge(own_v.sem, own_v.n)
            V.tensor_copy(R4[:, 0:NT * 8], ADR[:, :]).then_inc(own_v.sem, own_v.up())
            V.wait_ge(own_v.sem, own_v.n)
            V.tensor_scalar(R4[:, 32:64], R4[:, 0:32], float(-P), None, ALU.mult).then_inc(own_v.sem, own_v.up())
            V.wait_ge(own_v.sem, own_v.n)
            V.tensor_tensor(R4[:, 32:64], R4[:, 32:64], SL[:, :], ALU.add).then_inc(own_v.sem, own_v.up())
            V.wait_ge(own_v.sem, own_v.n)
            V.scalar_tensor_tensor(R4[:, 0:32], R4[:, 32:64], float(NBLK_PAD), R4[:, 0:32], ALU.mult, ALU.add).then_inc(own_v.sem, own_v.up())
            V.wait_ge(own_v.sem, own_v.n)
            V.tensor_copy(TOKI[:, :], K[:, BK_TOK:BK_TOK + NT]).then_inc(own_v.sem, own_v.up())
            V.wait_ge(own_v.sem, own_v.n)
            V.tensor_copy(ADR[:, :], R4[:, 0:32]).then_inc(ro_slots.sem, ro_slots.up())
            V.wait_ge(ro_slots.sem, 1)

        def positions_pe():
            pe_.wait_ge(ro_mask.sem, 1)
            for t in range(NT):
                for j in range(t + 1):
                    pe_.matmul(PS[:, 1, t * NE:(t + 1) * NE], strict if j == t else ones, mask[:, j * NE:(j + 1) * NE], start=j == 0, stop=j == t)
            for j in range(NT):
                mm = pe_.matmul(PS[:, 0, 0:NE], ones, mask[:, j * NE:(j + 1) * NE], start=j == 0, stop=j == NT - 1)
            mm.then_inc(ro_pos.sem, ro_pos.up())

        sg_mm, sg_silu, sg_a, sd_mm, sd_ev = (sig(n) for n in ("sg_mm", "sg_silu", "sg_a", "sd_mm", "sd_ev"))
        shw, shd = gu_w[0], dn_w[0]
        sa = GA[:, 0:2 * 512].rearrange("p (c t) -> p c t", c=2)
        sa_sig = GA[:, 1024:2048].rearrange("p (c t) -> p c t", c=2)

        def shared_pe():
            pe_.wait_ge(ld_sh.sem, 16 * 3)
            for c in range(2):
                for m in range(2):
                    for k in range(KD):
                        mm = pe_.matmul(PS[:, 2 + 2 * c + m, :], shw[:, k, m, c * P:(c + 1) * P], hT[:, k, :], start=k == 0, stop=k == KD - 1)
                mm.then_inc(sg_mm.sem, sg_mm.up())

        def shared_down_pe():
            pe_.wait_ge(sg_a.sem, 2)
            for n in range(2 * NT):
                t, half = n // 2, n % 2
                if n >= 2:
                    pe_.wait_ge(sd_ev.sem, n - 1)
                for c in range(2):
                    mm = pe_.matmul(PS[:, 6 + n % 2, :], sa[:, c, t * P:(t + 1) * P], shd[:, c, half * 512:(half + 1) * 512], start=c == 0, stop=c == 1)
                mm.then_inc(sd_mm.sem, sd_mm.up())

        def shared_act():
            for c in range(2):
                act_.wait_ge(sg_mm.sem, c + 1)
                act_.activation(sa_sig[:, c, :], PS[:, 2 + 2 * c, :], ACT.Silu).then_inc(sg_silu.sem, sg_silu.up())
            for n in range(2 * NT):
                act_.wait_ge(sd_mm.sem, n + 1)
                act_.activation(SH[:, n * 512:(n + 1) * 512], PS[:, 6 + n % 2, :], ACT.Copy).then_inc(sd_ev.sem, sd_ev.up())

        def shared_dve():
            for c in range(2):
                dve_.wait_ge(sg_silu.sem, c + 1)
                dve_.tensor_tensor(sa[:, c, :], sa_sig[:, c, :], PS[:, 3 + 2 * c, :], ALU.mult).then_inc(sg_a.sem, sg_a.up())

        ga_loaded = [sig(f"ga_loaded{r}") for r in range(UNROLL)]
        ix_set = [sig(f"ix_set{r}") for r in range(UNROLL)]
        y_stored = [sig(f"y_stored{r}") for r in range(UNROLL)]
        x_mm, x_ev, gu_mm, gu_silu, gu_a, at_mm, at_ev, dn_mm, dn_ev_a, dn_ev_v = (
            sig(n) for n in ("x_mm", "x_ev", "gu_mm", "gu_silu", "gu_a", "at_mm", "at_ev", "dn_mm", "dn_ev_a", "dn_ev_v"))
        y_zeroed = sig("y_zeroed")
        tabled, tab_loaded, tab_zero, tok_scattered = sig("tabled"), sig("tab_loaded"), sig("tab_zero"), sig("tok_scattered")
        primed, y_all = sig("primed"), sig("y_all")
        hg = [GT[:, i * D:(i + 1) * D].rearrange("p (k s) -> p k s", k=KD) for i in range(2)]
        U = UNROLL

        def trips(eng):
            n = eng.value_load(CI[0:1, 0:1], min_val=NE + U - 1, max_val=NBLK_PAD + U - 1)
            return n // U

        def sp_blocks(sp):
            sp.wait_ge(ro_slots.sem, 1)
            n = trips(sp)
            sp.wait_ge(sd_mm.sem, 2 * NT)
            with sp.Fori(0, n) as i:
                for r in range(U):
                    e = sp.value_load(CI[0:1, bass.ds(i * U + 4 + r, 1)], min_val=0, max_val=NE - 1)
                    sp.wait_ge(w_used[r].sem, i + 1)
                    for m, w in enumerate((w_gate, w_up)):
                        sp.dma_start(gu_w[r][:, :, m, :], w[bass.ds(e, 1), :, :].rearrange("o (k p) n -> p (o k) n", p=P)).then_inc(w_loaded[r].sem, 16)
                    sp.dma_start(dn_w[r], w_down[bass.ds(e, 1), :, :].rearrange("o (k p) n -> p (o k) n", p=P)).then_inc(w_loaded[r].sem, 16)

        def pool_blocks():
            n = trips(pool_)
            with pool_.Fori(0, n) as i:
                for r in range(U):
                    pool_.wait_ge(x_mm.sem, i * U + (r + 1))
                    pool_.tensor_copy(IDX[:, r:r + 1], TAB[:, bass.ds(i * U + r, 1)]).then_inc(ix_set[r].sem, 1)
                    pool_.wait_ge(ix_set[r].sem, i + 1)
                    pool_.nop(nofuse=True)
                    pool_.indirect_dma_start(out=GA[:, r * D:(r + 1) * D], out_offset=None, in_=h_rows,
                                             in_offset=bass.IndirectOffsetOnAxis(ap=IDX[:, r:r + 1].bitcast(U32), axis=0)).then_inc(ga_loaded[r].sem, 16)

        def pe_blocks():
            n = trips(pe_)
            with pe_.Fori(0, n) as i:
                def turn(r):
                    pe_.wait_ge(ga_loaded[r].sem, i * 16 + 16)
                    pe_.wait_ge(x_ev.sem, i * (2 * U) + 2 * r + 1)
                    for half in range(2):
                        for k in range(4):
                            mm = pe_.transpose(PS[:, half, k * P:(k + 1) * P], GA[:, r * D + (4 * half + k) * P:r * D + (4 * half + k + 1) * P], ident)
                    mm.then_inc(x_mm.sem, 1)

                def gate_up(r):
                    pe_.wait_ge(w_loaded[r].sem, i * 48 + 48)
                    pe_.wait_ge(x_ev.sem, i * (2 * U) + 2 * r + 3)
                    pe_.wait_ge(gu_a.sem, i * U + r + 1)
                    for k in range(KD):
                        mm = pe_.matmul(PS[:, 2, :], hg[r % 2][:, k, :], gu_w[r][:, k, :, :], start=k == 0, stop=k == KD - 1)
                    mm.then_inc(gu_mm.sem, 1)

                def turn_a(r):
                    pe_.wait_ge(gu_a.sem, i * U + r + 2)
                    pe_.wait_ge(at_ev.sem, i * U + r + 1)
                    for k in range(2):
                        mm = pe_.transpose(PS[:, 3, k * P:(k + 1) * P], SA[:, DE + k * P:DE + (k + 1) * P], ident)
                    mm.then_inc(at_mm.sem, 1)

                def down(r):
                    pe_.wait_ge(at_ev.sem, i * U + r + 2)
                    pe_.wait_ge(dn_ev_a.sem, i * U + r + 1)
                    pe_.wait_ge(dn_ev_v.sem, i * U + r + 1)
                    for half in range(2):
                        for k in range(2):
                            mm = pe_.matmul(PS[:, 4 + half, :], AT[:, (r % 2) * DE + k * P:(r % 2) * DE + (k + 1) * P], dn_w[r][:, k, half * 512:(half + 1) * 512],
                                            start=k == 0, stop=k == 1)
                        if half == 0:
                            mm.then_inc(dn_mm.sem, 1)
                    mm.then_inc(w_used[r].sem, 1)

                turn(0)
                for r in range(U):
                    gate_up(r)
                    if r + 1 < U:
                        turn(r + 1)
                    if r >= 1:
                        down(r - 1)
                    turn_a(r)
                down(U - 1)

        def act_blocks():
            act_.wait_ge(ro_slots.sem, 1)
            n = trips(act_)
            with act_.Fori(0, n) as i:
                def copy_x(r):
                    act_.wait_ge(x_mm.sem, i * U + U + r + 1)
                    act_.activation(GT[:, (r % 2) * D:(r % 2) * D + 512], PS[:, 0, :], ACT.Copy).then_inc(x_ev.sem, 1)
                copy_x(0)
                for r in range(U):
                    act_.wait_ge(gu_mm.sem, i * U + r + 1)
                    act_.activation(SA[:, 0:DE], PS[:, 2, 0:DE], ACT.Silu).then_inc(gu_silu.sem, 1)
                    if r + 1 < U:
                        copy_x(r + 1)
                    if r >= 1:
                        out_a(i, r - 1)
                out_a(i, U - 1)
            for r in range(U):
                act_.wait_ge(y_stored[r].sem, n * 16 + 16)
            act_.activation(S[:, 61:62], S[:, 0:1], ACT.Copy).then_inc(y_all.sem, y_all.up())

        def out_a(i, r):
            act_.wait_ge(dn_mm.sem, i * U + r + 1)
            act_.wait_ge(y_stored[r].sem, i * 16 + 16)
            act_.activation(YB[:, r * D:r * D + 512], PS[:, 4, :], ACT.Copy).then_inc(dn_ev_a.sem, 1)
            act_.wait_ge(dn_ev_a.sem, i * U + r + 2)
            act_.wait_ge(dn_ev_v.sem, i * U + r + 2)
            act_.dma_start(y_rows[bass.ds(i * (U * P) + r * P, P), :], YB[:, r * D:(r + 1) * D]).then_inc(y_stored[r].sem, 16)

        def dve_blocks():
            n = trips(dve_)
            with dve_.Fori(0, n) as i:
                def copy_x(r):
                    dve_.wait_ge(x_mm.sem, i * U + U + r + 1)
                    dve_.tensor_copy(GT[:, (r % 2) * D + 512:(r % 2) * D + 1024], PS[:, 1, :]).then_inc(x_ev.sem, 1)

                def copy_y(r):
                    dve_.wait_ge(w_used[r].sem, i + 2)
                    dve_.wait_ge(y_stored[r].sem, i * 16 + 16)
                    dve_.tensor_copy(YB[:, r * D + 512:(r + 1) * D], PS[:, 5, :]).then_inc(dn_ev_v.sem, 1)
                copy_x(0)
                for r in range(U):
                    dve_.wait_ge(gu_silu.sem, i * U + r + 1)
                    dve_.wait_ge(at_mm.sem, i * U + r + 1)
                    dve_.tensor_tensor(SA[:, DE:2 * DE], SA[:, 0:DE], PS[:, 2, DE:2 * DE], ALU.mult).then_inc(gu_a.sem, 1)
                    if r + 1 < U:
                        copy_x(r + 1)
                    if r >= 1:
                        copy_y(r - 1)
                    dve_.wait_ge(at_mm.sem, i * U + r + 2)
                    dve_.tensor_copy(AT[:, (r % 2) * DE:(r % 2 + 1) * DE], PS[:, 3, 0:DE]).then_inc(at_ev.sem, 1)
                copy_y(U - 1)

        g_loaded = [sig(f"g_loaded{r}") for r in range(4)]
        g_used = sig("g_used")
        added, scaled, final_s = sig("added"), sig("scaled"), sig("final_s")

        def combine_pool():
            pool_.wait_ge(y_all.sem, 1)
            for m in range(NT * TOP6):
                t, k = m // TOP6, m % TOP6
                if m >= 4:
                    pool_.wait_ge(g_used.sem, m - 3)
                pool_.indirect_dma_start(out=XN[:, (m % 4) * D:(m % 4 + 1) * D], out_offset=None, in_=y_rows,
                                         in_offset=bass.IndirectOffsetOnAxis(ap=SLI[:, t * 8 + k:t * 8 + k + 1].bitcast(U32), axis=0)).then_inc(g_loaded[m % 4].sem, g_loaded[m % 4].up(16))

        def combine_dve():
            dve_.wait_ge(sd_ev.sem, 2 * NT)
            for m in range(NT * TOP6):
                t, k = m // TOP6, m % TOP6
                dve_.wait_ge(g_loaded[m % 4].sem, 16 * (m // 4 + 1))
                dve_.scalar_tensor_tensor(sh3[:, t, :], XN[:, (m % 4) * D:(m % 4 + 1) * D], WK[:, t * 8 + k:t * 8 + k + 1], sh3[:, t, :],
                                          ALU.mult, ALU.add).then_inc(g_used.sem, g_used.up())
                dve_.wait_ge(g_used.sem, g_used.n)
                if k == TOP6 - 1:
                    dve_.tensor_tensor(sh3[:, t, :], sh3[:, t, :], GB[:, :], ALU.mult).then_inc(own_v.sem, own_v.up())
                    dve_.wait_ge(own_v.sem, own_v.n)
                    dve_.tensor_tensor(x3[:, t, :], x3[:, t, :], sh3[:, t, :], ALU.add).then_inc(added.sem, added.up())
            dve_.wait_ge(fin_rs.sem, 1)
            dve_.wait_ge(ld_row.sem, 16 * 3)
            for t in range(NT):
                dve_.scalar_tensor_tensor(x3[:, t, :], x3[:, t, :], rs[:, t:t + 1], GF[:, :], ALU.mult, ALU.mult).then_inc(final_s.sem, final_s.up())

        def combine_act():
            for t in range(NT):
                act_.wait_ge(added.sem, t + 1)
                act_.activation(HT[:, t * D:(t + 1) * D], x3[:, t, :], ACT.Square, accum_out=ms[:, t:t + 1]).then_inc(fin_sq.sem, fin_sq.up())
            act_.wait_ge(fin_sq.sem, NT)
            act_.activation(rs, ms[:, 0:NT], ACT.Ln, scale=1.0 / D, bias=EPS).then_inc(own_a.sem, own_a.up())
            act_.wait_ge(own_a.sem, own_a.n)
            act_.activation(rs, rs, ACT.Exp, scale=-0.5).then_inc(fin_rs.sem, fin_rs.up())

        block = ctx.enter_context(nc.Block())

        @block.sync
        def _(sp):
            def cols(w, a, b):
                return w.rearrange("(k p) n -> p k n", p=P)[:, :, a:b]
            sp.dma_start(K[:, :], consts).then_inc(ld_const.sem, ld_const.up(16))
            sp.dma_start(VR[0:16, :], b_mod[3 * D:5 * D].rearrange("(r p) -> r p", p=P)).then_inc(ld_vec.sem, ld_vec.up(16))
            sp.dma_start(VR[16:24, :], g_ffn.rearrange("(r p) -> r p", p=P)).then_inc(ld_vec.sem, ld_vec.up(16))
            sp.dma_start(VR[24:40, :], mod[0:2 * D].rearrange("(r p) -> r p", p=P)).then_inc(ld_vec.sem, ld_vec.up(16))
            sp.dma_start(x3, x_in.rearrange("(t p) d -> p t d", p=P)).then_inc(ld_x.sem, ld_x.up(16))
            sp.dma_start(rw, router_w.rearrange("(k p) e -> p k e", p=P)).then_inc(ld_rw.sem, ld_rw.up(16))
            for dst, src, landed in ((RB, router_bias, ld_rw), (GF, g_final, ld_row), (GB, mod[2 * D:3 * D], ld_row),
                                     (GA, b_mod[5 * D:6 * D], ld_row)):
                n = src.shape[0]
                sp.dma_start(dst[:, 0:n], src.rearrange("(a n) -> a n", a=1).to_broadcast([P, n])).then_inc(landed.sem, landed.up(16))
            for m, w in enumerate((s_gate, s_up)):
                sp.dma_start(shw[:, :, m, :], w.rearrange("(k p) n -> p k n", p=P)).then_inc(ld_sh.sem, ld_sh.up(16))
            sp.dma_start(shd, s_down.rearrange("(k p) n -> p k n", p=P)).then_inc(ld_sh.sem, ld_sh.up(16))
            sp.wait_ge(rturn.copied.sem, 2 * NT)
            sp.dma_start(h_rows.rearrange("(t p) d -> p t d", p=P), xn).then_inc(rows_stored.sem, rows_stored.up(16))
            sp_blocks(sp)
            sp.wait_ge(final_s.sem, NT)
            sp.dma_start(x_out.rearrange("(t p) d -> p t d", p=P), x3).then_inc(stored.sem, stored.up(16))
            sp.wait_ge(stored.sem, 16)

        @block.gpsimd
        def _(pool):
            pool.memset(TAB[:, :], 0).then_inc(tab_zero.sem, tab_zero.up())
            pool.memset(YB[:, 0:D], 0.0).then_inc(tab_zero.sem, tab_zero.up())
            pool.wait_ge(tab_zero.sem, 2)
            pool.dma_start(y_rows[NE * P:NBLK_PAD * P, :].rearrange("(b p) d -> p b d", p=P),
                           YB[:, 0:D].rearrange("p (o d) -> p o d", o=1).to_broadcast([P, NBLK_PAD - NE, D])).then_inc(y_zeroed.sem, y_zeroed.up(16))
            pool.dma_start(slot_tok.rearrange("(p b) o -> p (b o)", p=P), TAB[:, :]).then_inc(tabled.sem, tabled.up(16))
            pool.wait_ge(tabled.sem, 16)
            pool.wait_ge(ro_slots.sem, 1)
            for t in range(NT):
                for k in range(TOP6):
                    pool.indirect_dma_start(out=slot_tok, out_offset=bass.IndirectOffsetOnAxis(ap=ADR[:, t * 8 + k:t * 8 + k + 1].bitcast(U32), axis=0),
                                            in_=TOKI[:, t:t + 1], in_offset=None).then_inc(tok_scattered.sem, tok_scattered.up(16))
            pool.wait_ge(tok_scattered.sem, 16 * NT * TOP6)
            pool.dma_start(TAB[:, :], slot_tok.rearrange("(p b) o -> p (b o)", p=P)).then_inc(tab_loaded.sem, tab_loaded.up(16))
            pool.wait_ge(tab_loaded.sem, 16)
            pool.wait_ge(rows_stored.sem, 16)
            pool.wait_ge(y_zeroed.sem, 16)
            pool.wait_ge(sg_a.sem, 2)
            pool.wait_ge(sd_mm.sem, 2 * NT)
            pool_blocks()
            combine_pool()

        @block.tensor
        def _(pe):
            vec_pe()
            norm_pe()
            router_pe()
            pe.wait_ge(rturn.copied.sem, 2 * NT)
            shared_pe()
            positions_pe()
            shared_down_pe()
            pe.wait_ge(ro_slots.sem, 1)
            pe.wait_ge(gb_ready.sem, 1)
            pe.wait_ge(sd_ev.sem, 2 * NT)
            pe.wait_ge(primed.sem, 1)
            pe_blocks()

        @block.scalar
        def _(act):
            norm_act()
            router_act()
            shared_act()
            act_blocks()
            combine_act()

        @block.vector
        def _(dve):
            mod_dve()
            norm_dve()
            gate_dve()
            router_dve()
            for s_, by in [(x_mm, U), (x_ev, 1), (gu_a, 1), (at_ev, 1), (at_mm, 1), (dn_ev_a, 1), (dn_ev_v, 1)] + [(w, 1) for w in w_used] + [(y, 16) for y in y_stored]:
                dve.sem_inc(s_.sem, by)
            dve.tensor_copy(S[:, 60:61], S[:, 0:1]).then_inc(primed.sem, primed.up())
            dve_blocks()
            combine_dve()


L2_HEADS = 4
HD = 64
IH = 8
FF = 4 * D
NFF = FF // P
CH = 64
TOPK = min(256, T // 4)
RING = 2
A_Q, A_K, A_V, A_QI, A_KI, A_WI = 0, 256, 320, 384, 896, 960
B_Q, B_K, B_V, B_G = 968, 1224, 1480, 1736
C_Q, C_K, C_V, C_A, C_G = 1992, 2120, 2248, 2504, 2520
D_Q, D_K, D_V = 2776, 3032, 3288
SEGS = [(0, 512), (512, 968), (968, 1480), (1480, 1992), (2248, 2504), (2520, 2776), (2776, 3288), (3288, 3544)]
PW = sum(b - a for a, b in SEGS)


def at(col):
    o = 0
    for a, b in SEGS:
        if a <= col < b:
            return o + col - a
        o += b - a
    raise ValueError(col)


NFREQ = 40
LEVELS = 6
K_ID, K_MASK, K_D = 0, P, P + LEVELS * P
K_SCAN = K_D + L2_HEADS * T
K_INV = K_SCAN + T
K_NEG = K_INV + NFREQ
K_ONE = K_NEG + P
K_COLS = K_ONE + P


def layer_constants():
    c = np.zeros((P, K_COLS), np.float32)
    i = np.arange(P)
    c[:, K_ID:K_ID + P] = np.eye(P)
    for l in range(LEVELS):
        blk, half = i >> (l + 1), (i >> l) & 1
        c[:, K_MASK + l * P:K_MASK + (l + 1) * P] = (blk[:, None] == blk[None]) & (half[:, None] != half[None])
    q = np.arange(T)
    for h in range(L2_HEADS):
        g = 1.0 - 2.0 ** (-5.0 - h)
        dist = q[None] - i[:, None]
        same = (q[None] // CH) == (i[:, None] // CH)
        later = (q[None] // CH) > (i[:, None] // CH)
        val = np.where(same, g ** np.abs(dist), np.where(later, g ** np.maximum(dist, 0), 0.0))
        c[:, K_D + h * T:K_D + (h + 1) * T] = val * HD ** -0.5
    c[:, K_SCAN:K_SCAN + T] = (q % CH != 0)[None]
    f32 = np.float32
    for o, half, theta in ((0, 32, 10000.0), (32, 8, 500000.0)):
        e = (-np.arange(half, dtype=f32) / f32(half)).astype(f32)
        c[:, K_INV + o:K_INV + o + half] = np.power(f32(theta), e)
    c[::32, K_NEG:K_NEG + CH] = NEG
    c[::32, K_ONE:K_ONE + P] = 1.0
    return c


R_MODB, R_PRE1, R_PRE2, R_C, R_BA, R_MOD, R_ALL = 0, 48, 56, 64, 72, 73, 121


def layer(nc, l, x_in, x_out, c_2, positions, mod, next_mod_w, next_mod, mod_b, pre1_g, post1_g, pre2_g, post2_g, w_in,
          wa2, ba, lq1, lk1, lq2, lk2, hn_g, w_out, w1, w2, consts):
    lam_init = 0.8 - 0.6 * float(np.exp(-0.3 * l))
    pe_, act_, dve_, pool_ = nc.tensor, nc.scalar, nc.vector, nc.gpsimd
    with Scope(nc) as ctx:
        def sb(name, cols, parts=P, dt=F32):
            return ctx.enter_context(nc.sbuf_tensor(f"{name}_{l}", [parts, cols], dt))

        def sig(name):
            return Signal(ctx, nc, f"{name}_{l}")

        X = sb("x", NT * D)
        HT = sb("hT", KD * T)
        AR = sb("arena", PW * NT + 12 * T)
        ring = sb("ring", RING * 8 * 512)
        PT = sb("pT", 4 * 4 * P)
        SM = sb("work", 2048)
        NB = sb("notsel", NT * T)
        K = sb("consts", K_COLS)
        GR = sb("gates", 2 * D)
        HNG = sb("hng", D)
        CS = sb("cossin", 2 * NT * NFREQ)
        VR = sb("vrows", P)
        VC = sb("vcols", R_ALL)
        MC = sb("modcols", 48)
        GL = sb("gla", 3 * T)
        QD = sb("qdkd", 2 * T)
        S = sb("small", 256)
        WA = sb("wa2", P)
        POS = sb("pos", NT, dt=I32)
        PS = ctx.enter_context(nc.psum_tensor(f"ps_{l}", [P, 8, 512], F32))

        x3 = X[:, :].rearrange("p (t d) -> p t d", t=NT)
        hT = HT[:, :].rearrange("p (k t) -> p k t", k=KD)
        proj = AR[:, 0:PW * NT].rearrange("p (t c) -> p t c", t=NT)
        TB = AR[:, PW * NT:PW * NT + 12 * T].rearrange("p (b t) -> p b t", b=12)
        xn = AR[:, 0:NT * D].rearrange("p (t d) -> p t d", t=NT)
        fT = AR[:, 0:NFF * T].rearrange("p (m t) -> p m t", m=NFF)
        pT = PT[:, :].rearrange("p (j h q) -> p j h q", j=4, h=4)
        kdup = PT[:, 0:NT * 256].rearrange("p (t c) -> p t c", t=NT)
        sm = SM[:, :].rearrange("p (h s) -> p h s", h=4)
        nb = NB[:, :].rearrange("p (t s) -> p t s", t=NT)
        ident = K[:, K_ID:K_ID + P]
        dtab = K[:, K_D:K_D + 4 * T].rearrange("p (h q) -> p h q", h=4)
        ones = K[0:1, K_ONE:K_ONE + P]
        cosv = CS[:, 0:NT * NFREQ].rearrange("p (t f) -> p t f", t=NT)
        sinv = CS[:, NT * NFREQ:].rearrange("p (t f) -> p t f", t=NT)
        cos_all, sin_all = CS[:, 0:NT * NFREQ], CS[:, NT * NFREQ:]
        qT, kT, bT = GL[:, 0:T], GL[:, T:2 * T], GL[:, 2 * T:3 * T]
        qd, kd = QD[:, 0:T], QD[:, T:2 * T]
        ms, rs = S[:, 0:8], S[:, 8:12]
        mx, sumc, rec = S[:, 16:24], S[:, 24:32], S[:, 32:40]
        mean, var = S[:, 40:56], S[:, 56:72]
        lam = S[:, 88:92]
        gl8 = S[:, 96:104]
        top = S[:, 104:112]
        csc, cse = S[:, 120:128], S[:, 128:136]
        ones_col = S[:, 200:201]
        posf = S[:, 136:140]
        wis = S[:, 144:176].rearrange("p (t h) -> p t h", t=NT)
        states = [proj[:, c // 2, at(A_QI) + (c % 2) * 256:at(A_QI) + (c % 2) * 256 + 256] for c in range(8)]
        own_v, own_a, own_g = sig("dve"), sig("act"), sig("pool")

        def cols(w, a, b):
            return w.rearrange("(k p) n -> p k n", p=P)[:, :, a:b]

        def rows(w, m):
            return w[m * 4 * P:(m + 1) * 4 * P, :].rearrange("(k p) n -> p k n", p=P)

        tiles = [cols(w_in, a, b) for a, b in SEGS]
        tiles += [cols(w_in, C_Q, C_K + 128), cols(w_in, C_A, C_A + 16)]
        tiles += [rows(w_out, m) for m in range(2)]
        tiles += [cols(w1, t * 512, (t + 1) * 512) for t in range(8)]
        tiles += [rows(w2, m) for m in range(8)]
        w_loaded = [sig(f"w_loaded{r}") for r in range(RING)]
        w_used = sig("w_used")
        taken, owed = [0], [False]

        def product(out, lhsT, rhs, start, stop):
            mm = pe_.matmul(out, lhsT, rhs, start=start, stop=stop)
            if owed[0]:
                owed[0] = False
                mm.then_inc(w_used.sem, w_used.up())
            return mm

        def slot(n):
            k, w = tiles[n].shape[1], tiles[n].shape[2]
            return ring[:, (n % RING) * 4096:(n % RING) * 4096 + k * w].rearrange("p (k n) -> p k n", k=k)

        def take():
            n = taken[0]
            taken[0] += 1
            owed[0] = n > w_used.n
            pe_.wait_ge(w_loaded[n % RING].sem, 16 * (n // RING + 1))
            return slot(n)

        ld_const, ld_x, ld_vec, ld_row, ld_gate, ld_hng = sig("ld_const"), sig("ld_x"), sig("ld_vec"), sig("ld_row"), sig("ld_gate"), sig("ld_hng")
        stored = sig("stored")
        N_ROWS = 6

        def loads_sp(sp):
            sp.dma_start(K[:, :], consts).then_inc(ld_const.sem, ld_const.up(16))
            for r0, src in ((R_MODB, mod_b), (R_PRE1, pre1_g), (R_PRE2, pre2_g), (R_C, c_2), (R_BA, ba), (R_MOD, mod)):
                n = src.shape[0] // P
                sp.dma_start(VR[r0:r0 + n, :], src.rearrange("(r p) -> r p", p=P)).then_inc(ld_vec.sem, ld_vec.up(16))
            for dst, row in ((SM[0:1, 0:32], lq1), (SM[0:1, 32:64], lk1), (SM[0:1, 64:96], lq2), (SM[0:1, 96:128], lk2)):
                sp.dma_start(dst, row.rearrange("(a n) -> a n", a=1)).then_inc(ld_row.sem, ld_row.up(16))
            sp.dma_start(POS[:, :], positions.rearrange("(t p) -> p t", p=P), allow_slow_non_contiguous=True).then_inc(ld_row.sem, ld_row.up(16))
            sp.dma_start(WA[0:16, :], wa2).then_inc(ld_row.sem, ld_row.up(16))
            sp.dma_start(x3, x_in.rearrange("(t p) d -> p t d", p=P)).then_inc(ld_x.sem, ld_x.up(16))
            for dst, row in ((GR[:, 0:D], mod[2 * D:3 * D]), (GR[:, D:2 * D], mod[5 * D:6 * D]),
                             (NB[:, 0:D], mod_b[2 * D:3 * D]), (NB[:, D:2 * D], mod_b[5 * D:6 * D]),
                             (PT[:, 0:D], post1_g), (PT[:, D:2 * D], post2_g)):
                sp.dma_start(dst, row.rearrange("(a n) -> a n", a=1).to_broadcast([P, D])).then_inc(ld_gate.sem, ld_gate.up(16))
            sp.dma_start(HNG[:, :], hn_g.rearrange("(a n) -> a n", a=1).to_broadcast([P, D])).then_inc(ld_hng.sem, ld_hng.up(16))

        vec_turned, vec_cols, silu_e, silu = sig("vec_turned"), sig("vec_cols"), sig("silu_e"), sig("silu")

        def cond_pe():
            pe_.wait_ge(ld_const.sem, 16)
            pe_.wait_ge(ld_vec.sem, 16 * 6)
            pe_.transpose(PS[:, 0, 0:R_ALL], VR[0:R_ALL, :], ident[0:R_ALL, 0:R_ALL]).then_inc(vec_turned.sem, vec_turned.up())

        def cond_act():
            act_.wait_ge(vec_cols.sem, 1)
            act_.activation(cse, VC[:, R_C:R_C + 8], ACT.Exp, scale=-1.0).then_inc(silu_e.sem, silu_e.up())

        def cond_dve():
            dve_.wait_ge(vec_turned.sem, 1)
            dve_.tensor_copy(VC[:, :], PS[:, 0, 0:R_ALL]).then_inc(vec_cols.sem, vec_cols.up())
            if next_mod is None:
                return
            dve_.memset(ones_col, 1.0).then_inc(silu.sem, silu.up())
            dve_.wait_ge(silu_e.sem, 1)
            dve_.tensor_scalar(cse, cse, 1.0, None, ALU.add).then_inc(own_v.sem, own_v.up())
            dve_.wait_ge(own_v.sem, own_v.n)
            dve_.reciprocal(cse, cse).then_inc(own_v.sem, own_v.up())
            dve_.wait_ge(own_v.sem, own_v.n)
            dve_.tensor_tensor(csc, cse, VC[:, R_C:R_C + 8], ALU.mult).then_inc(silu.sem, silu.up())

        mod_cols, gates_ready = sig("mod_cols"), sig("gates_ready")

        def mod_dve():
            dve_.wait_ge(vec_cols.sem, 1)
            dve_.tensor_tensor(MC[:, :], VC[:, R_MOD:R_MOD + 48], VC[:, 0:48], ALU.add).then_inc(own_v.sem, own_v.up())
            dve_.wait_ge(own_v.sem, own_v.n)
            for sc, g in ((8, R_PRE1), (32, R_PRE2)):
                dve_.scalar_tensor_tensor(MC[:, sc:sc + 8], MC[:, sc:sc + 8], 1.0, VC[:, g:g + 8], ALU.add, ALU.mult).then_inc(mod_cols.sem, mod_cols.up())

        def gates_dve():
            dve_.wait_ge(ld_gate.sem, 16 * 6)
            dve_.tensor_tensor(GR[:, :], GR[:, :], NB[:, :], ALU.add).then_inc(own_v.sem, own_v.up())
            dve_.wait_ge(own_v.sem, own_v.n)
            dve_.tensor_tensor(GR[:, :], GR[:, :], PT[:, :], ALU.mult).then_inc(gates_ready.sem, gates_ready.up())

        lam_s, lam_e, lam_row, lam_mm, lam_ready = sig("lam_s"), sig("lam_e"), sig("lam_row"), sig("lam_mm"), sig("lam_ready")

        def lam_dve():
            dve_.wait_ge(ld_row.sem, 16 * N_ROWS)
            for n in range(2):
                dve_.tensor_tensor_reduce(SM[0:1, n * 64:n * 64 + 32], SM[0:1, n * 64:n * 64 + 32], SM[0:1, n * 64 + 32:n * 64 + 64],
                                          1.0, 0.0, ALU.mult, ALU.add, lam[0:1, n:n + 1]).then_inc(lam_s.sem, lam_s.up())
            dve_.wait_ge(lam_e.sem, 1)
            dve_.tensor_tensor(lam[0:1, 2:3], lam[0:1, 1:2], lam[0:1, 0:1], ALU.subtract).then_inc(own_v.sem, own_v.up())
            dve_.wait_ge(own_v.sem, own_v.n)
            dve_.tensor_scalar(lam[0:1, 2:3], lam[0:1, 2:3], -lam_init, None, ALU.add).then_inc(lam_row.sem, lam_row.up())
            dve_.wait_ge(lam_mm.sem, 1)
            dve_.tensor_copy(lam[:, 3:4], PS[:, 6, 0:1]).then_inc(lam_ready.sem, lam_ready.up())

        def lam_act():
            act_.wait_ge(lam_s.sem, 2)
            act_.activation(lam[0:1, 0:2], lam[0:1, 0:2], ACT.Exp).then_inc(lam_e.sem, lam_e.up())

        def lam_pe():
            pe_.wait_ge(lam_row.sem, 1)
            pe_.matmul(PS[:, 6, 0:1], ones, lam[0:1, 2:3], start=True, stop=True).then_inc(lam_mm.sem, lam_mm.up())

        ang_ready, trig = sig("ang_ready"), sig("trig")
        TWO_PI = 2 * np.pi
        C1 = 6.28125
        C2 = float(np.float32(np.round((TWO_PI - C1) * 2 ** 20) / 2 ** 20))
        C3 = float(TWO_PI - C1 - C2)
        MAGIC = 1.5 * 2 ** 23
        TOP = 3.1415925

        def trig_dve():
            dve_.wait_ge(ld_const.sem, 16)
            dve_.tensor_copy(posf, POS[:, :]).then_inc(own_v.sem, own_v.up())
            dve_.wait_ge(own_v.sem, own_v.n)
            for t in range(NT):
                dve_.tensor_scalar(sinv[:, t, :], K[:, K_INV:K_INV + NFREQ], posf[:, t:t + 1], None, ALU.mult).then_inc(own_v.sem, own_v.up())
            dve_.wait_ge(own_v.sem, own_v.n)
            turns = cos_all
            dve_.tensor_scalar(turns, sin_all, 1.0 / TWO_PI, MAGIC, ALU.mult, ALU.add).then_inc(own_v.sem, own_v.up())
            dve_.wait_ge(own_v.sem, own_v.n)
            dve_.tensor_scalar(turns, turns, MAGIC, None, ALU.subtract).then_inc(own_v.sem, own_v.up())
            dve_.wait_ge(own_v.sem, own_v.n)
            for c in (C1, C2, C3):
                dve_.scalar_tensor_tensor(sin_all, turns, -c, sin_all, ALU.mult, ALU.add).then_inc(own_v.sem, own_v.up())
                dve_.wait_ge(own_v.sem, own_v.n)
            dve_.tensor_scalar(cos_all, sin_all, float(np.pi / 2), -TWO_PI, ALU.is_gt, ALU.mult).then_inc(own_v.sem, own_v.up())
            dve_.wait_ge(own_v.sem, own_v.n)
            dve_.scalar_tensor_tensor(cos_all, sin_all, float(np.pi / 2), cos_all, ALU.add, ALU.add).then_inc(own_v.sem, own_v.up())
            dve_.wait_ge(own_v.sem, own_v.n)
            dve_.tensor_scalar(cos_all, cos_all, TOP, -TOP, ALU.min, ALU.max).then_inc(ang_ready.sem, ang_ready.up())
            dve_.tensor_scalar(sin_all, sin_all, TOP, -TOP, ALU.min, ALU.max).then_inc(ang_ready.sem, ang_ready.up())

        def trig_act():
            act_.wait_ge(ang_ready.sem, 2)
            act_.activation(sin_all, sin_all, ACT.Sin).then_inc(trig.sem, trig.up())
            act_.activation(cos_all, cos_all, ACT.Sin).then_inc(trig.sem, trig.up())

        class Normed:
            def __init__(self, name, scale, shift, x_signal, x_step):
                self.sq, self.rs, self.xn = sig(name + "_sq"), sig(name + "_rs"), sig(name + "_xn")
                self.turn = Turn(nc, ctx, f"{name}_{l}", [PS[:, b, :] for b in (0, 1, 2, 3)], ident)
                self.scale, self.shift, self.x_signal, self.x_step = scale, shift, x_signal, x_step

            def act(self):
                for t in range(NT):
                    act_.wait_ge(self.x_signal.sem, 16 if self.x_step == 0 else self.x_step * (t + 1))
                    act_.activation(HT[:, t * D:(t + 1) * D], x3[:, t, :], ACT.Square, accum_out=ms[:, t:t + 1]).then_inc(self.sq.sem, self.sq.up())
                act_.wait_ge(self.sq.sem, NT)
                act_.activation(rs, ms[:, 0:NT], ACT.Ln, scale=1.0 / D, bias=EPS).then_inc(own_a.sem, own_a.up())
                act_.wait_ge(own_a.sem, own_a.n)
                act_.activation(rs, rs, ACT.Exp, scale=-0.5).then_inc(self.rs.sem, self.rs.up())

            def dve(self):
                dve_.wait_ge(self.rs.sem, 1)
                for t in range(NT):
                    dve_.tensor_scalar(xn[:, t, :], x3[:, t, :], rs[:, t:t + 1], None, ALU.mult).then_inc(self.xn.sem, self.xn.up())
                dve_.wait_ge(mod_cols.sem, 2)
                for k in range(KD):
                    bank = self.turn.bank(dve_)
                    dve_.tensor_scalar(hT[:, k, :], bank, MC[:, self.scale + k:self.scale + k + 1],
                                       MC[:, self.shift + k:self.shift + k + 1], ALU.mult, ALU.add).then_inc(self.turn.copied.sem, self.turn.copied.up())

            def pe(self):
                pe_.wait_ge(self.xn.sem, NT)
                for k in range(KD):
                    self.turn.pe([(xn[:, t, k * P:(k + 1) * P], slice(t * P, (t + 1) * P)) for t in range(NT)])
                pe_.wait_ge(self.turn.copied.sem, KD)

        pr_mm, pr_ev, cm_mm, cm_ev, low_mm = sig("pr_mm"), sig("pr_ev"), sig("cm_mm"), sig("cm_ev"), sig("low_mm")

        def proj_pe():
            for s, (a, b) in enumerate(SEGS):
                w = take()
                for t in range(NT):
                    if s >= 2:
                        pe_.wait_ge(pr_ev.sem, 4 * (s - 2) + t + 1)
                    for k in range(KD):
                        mm = product(PS[:, 4 * (s % 2) + t, 0:b - a], hT[:, k, t * P:(t + 1) * P], w[:, k, :],
                                        start=k == 0, stop=k == KD - 1)
                    mm.then_inc(pr_mm.sem, pr_mm.up())
            w = take()
            pe_.wait_ge(pr_ev.sem, 4 * (len(SEGS) - 1))
            for n in range(2):
                for k in range(KD):
                    mm = product(PS[:, n, :], w[:, k, n * P:(n + 1) * P], hT[:, k, :], start=k == 0, stop=k == KD - 1)
                mm.then_inc(cm_mm.sem, cm_mm.up())
            w = take()
            for k in range(KD):
                mm = product(PS[0:16, 2, :], w[:, k, :], hT[:, k, :], start=k == 0, stop=k == KD - 1)
            mm.then_inc(cm_mm.sem, cm_mm.up())
            pe_.wait_ge(cm_ev.sem, 3)
            pe_.matmul(PS[:, 3, :], WA[0:16, :], QD[0:16, 0:T], start=True, stop=True).then_inc(w_used.sem, w_used.up())
            low_tiles = w_used.n
            assert low_tiles == taken[0] == N_LOW

        log_a = sig("log_a")
        N_LOW = len(SEGS) + 2

        def proj_act():
            for s, (a, b) in enumerate(SEGS):
                o = at(a)
                for t in range(NT):
                    act_.wait_ge(pr_mm.sem, 4 * s + t + 1)
                    act_.activation(proj[:, t, o:o + b - a], PS[:, 4 * (s % 2) + t, 0:b - a], ACT.Copy).then_inc(pr_ev.sem, pr_ev.up())
            act_.wait_ge(cm_mm.sem, 1)
            act_.activation(qT, PS[:, 0, :], ACT.Copy, scale=float(np.float32(32.0 ** -0.5))).then_inc(cm_ev.sem, cm_ev.up())
            act_.wait_ge(cm_mm.sem, 2)
            act_.activation(kT, PS[:, 1, :], ACT.Copy).then_inc(cm_ev.sem, cm_ev.up())
            act_.wait_ge(cm_mm.sem, 3)
            act_.activation(QD[0:16, 0:T], PS[0:16, 2, :], ACT.Copy).then_inc(cm_ev.sem, cm_ev.up())
            act_.wait_ge(w_used.sem, N_LOW)
            act_.activation(bT, PS[:, 3, :], ACT.Abs, bias=VC[:, R_BA:R_BA + 1]).then_inc(own_a.sem, own_a.up())
            act_.wait_ge(own_a.sem, own_a.n)
            act_.activation(bT, bT, ACT.Exp, scale=-1.0).then_inc(own_a.sem, own_a.up())
            act_.wait_ge(own_a.sem, own_a.n)
            act_.activation(bT, bT, ACT.Ln, bias=1.0).then_inc(log_a.sem, log_a.up())

        b_ready, ex_ready = sig("b_ready"), sig("ex_ready")
        eb, el = NB[:, 0:T], NB[:, T:2 * T]

        def decay_dve():
            dve_.wait_ge(log_a.sem, 1)
            dve_.tensor_scalar(SM[:, 0:T], PS[:, 3, :], VC[:, R_BA:R_BA + 1], 0.0, ALU.add, ALU.min).then_inc(own_v.sem, own_v.up())
            dve_.wait_ge(own_v.sem, own_v.n)
            dve_.tensor_tensor(SM[:, 0:T], SM[:, 0:T], bT, ALU.subtract).then_inc(own_v.sem, own_v.up())
            dve_.wait_ge(own_v.sem, own_v.n)
            dve_.tensor_scalar(SM[:, 0:T], SM[:, 0:T], 1.0 / 16.0, None, ALU.mult).then_inc(own_v.sem, own_v.up())
            dve_.wait_ge(own_v.sem, own_v.n)
            dve_.tensor_tensor_scan(bT, K[:, K_SCAN:K_SCAN + T], SM[:, 0:T], 0.0, ALU.mult, ALU.add).then_inc(b_ready.sem, b_ready.up())

        rope_a, rope_bd, dup = sig("rope_a"), sig("rope_bd"), sig("dup")
        ROPE_A = [(at(A_Q), 5, 64, 8, 32, 1), (at(A_QI), 9, 64, 8, 32, 1)]
        ROPE_BD = [(at(B_Q), 8, 64, 32, 0, 1), (at(D_Q), 16, 32, 4, 32, 2)]

        def rope(e, groups, signal, own, scratch):
            e.wait_ge(trig.sem, 2)
            e.wait_ge(pr_ev.sem, 4 * len(SEGS))
            for t in range(NT):
                for col, heads, width, half, f0, fstep in groups:
                    v = proj[:, t, col:col + heads * width].rearrange("p (h w) -> p h w", h=heads)
                    x1, x2 = v[:, :, 0:half], v[:, :, half:2 * half]
                    w = [scratch[:, i * 256:i * 256 + heads * half].rearrange("p (h w) -> p h w", h=heads) for i in range(2)]
                    fs = slice(f0, f0 + half * fstep, fstep)
                    c_ = cosv[:, t:t + 1, fs].to_broadcast([P, heads, half])
                    s_ = sinv[:, t:t + 1, fs].to_broadcast([P, heads, half])
                    e.tensor_tensor(w[0], x1, s_, ALU.mult).then_inc(own.sem, own.up())
                    e.tensor_tensor(w[1], x2, s_, ALU.mult).then_inc(own.sem, own.up())
                    e.wait_ge(own.sem, own.n)
                    e.tensor_tensor(x1, x1, c_, ALU.mult).then_inc(own.sem, own.up())
                    e.tensor_tensor(x2, x2, c_, ALU.mult).then_inc(own.sem, own.up())
                    e.wait_ge(own.sem, own.n)
                    e.tensor_tensor(x1, x1, w[1], ALU.subtract).then_inc(signal.sem, signal.up())
                    e.tensor_tensor(x2, x2, w[0], ALU.add).then_inc(signal.sem, signal.up())
                    e.wait_ge(signal.sem, signal.n)

        def dup_pool():
            pool_.wait_ge(rope_a.sem, 2 * 2 * NT)
            for n, col in enumerate((A_K, A_K, A_KI, A_KI)):
                pool_.tensor_copy(kdup[:, :, n * 64:n * 64 + 64], proj[:, :, at(col):at(col) + 64]).then_inc(dup.sem, dup.up())

        qk = Turn(nc, ctx, f"qk_{l}", [PS[:, 4 + b, :] for b in range(4)], ident)
        BLK = [(proj, at(A_Q)), (proj, at(A_Q) + 128), (proj, at(A_QI)), (proj, at(A_QI) + 128), (proj, at(A_QI) + 256),
               (proj, at(A_QI) + 384), (kdup, 0), (kdup, 128), (proj, at(B_Q)), (proj, at(B_Q) + 128), (proj, at(B_K)),
               (proj, at(B_K) + 128), (proj, at(D_Q)), (proj, at(D_Q) + 128), (proj, at(D_K)), (proj, at(D_K) + 128)]

        def qk_pe(first, last):
            for src, col in BLK[first:last]:
                qk.pe([(src[:, t, col:col + P], slice(t * P, (t + 1) * P)) for t in range(NT)])

        def qk_act(first, last):
            for b in range(first, last):
                bank = qk.bank(act_)
                act_.activation(TB[:, b % 12, :], bank, ACT.Copy).then_inc(qk.copied.sem, qk.copied.up())

        ix_mm, ix_relu, ix_acc, nb_ready = sig("ix_mm"), sig("ix_relu"), sig("ix_acc"), sig("nb_ready")
        relu2 = [SM[:, 0:512], SM[:, 512:1024]]
        score = SM[:, 1024:1536]

        def index_pe():
            pe_.wait_ge(b_ready.sem, 1)
            pe_.wait_ge(qk.copied.sem, 8)
            for i in range(1, NT):
                s = (i + 1) * P
                for h in range(IH):
                    n, o = ix_mm.n, (h % 2) * 64
                    if n >= 4:
                        pe_.wait_ge(ix_relu.sem, n - 3)
                    pe_.matmul(PS[:, n % 4, 0:s], TB[o:o + 64, 2 + h // 2, i * P:(i + 1) * P], TB[o:o + 64, 7, 0:s],
                               start=True, stop=True).then_inc(ix_mm.sem, ix_mm.up())

        def index_act():
            act_.wait_ge(b_ready.sem, 1)
            for n in range(3 * IH):
                s = (n // IH + 2) * P
                act_.wait_ge(ix_mm.sem, n + 1)
                if n >= 2:
                    act_.wait_ge(ix_acc.sem, n - 1)
                act_.activation(relu2[n % 2][:, 0:s], PS[:, n % 4, 0:s], ACT.Relu).then_inc(ix_relu.sem, ix_relu.up())

        def index_dve():
            dve_.tensor_scalar(wis, proj[:, :, at(A_WI):at(A_WI) + IH], float(IH ** -0.5 * HD ** -0.5), None, ALU.mult).then_inc(own_v.sem, own_v.up())
            dve_.wait_ge(own_v.sem, own_v.n)
            dve_.wait_ge(rope_bd.sem, 4 * NT)
            dve_.memset(nb[:, 0, 0:P], 0.0).then_inc(own_v.sem, own_v.up())
            dve_.wait_ge(own_v.sem, own_v.n)
            dve_.memset(nb[0:CH, 0, CH:P], NEG).then_inc(nb_ready.sem, nb_ready.up())
            for i in range(1, NT):
                s = (i + 1) * P
                for h in range(IH):
                    n = ix_acc.n
                    dve_.wait_ge(ix_relu.sem, n + 1)
                    wh, r = wis[:, i, h:h + 1], relu2[n % 2][:, 0:s]
                    if h == 0:
                        dve_.tensor_scalar(nb[:, i, 0:s], r, wh, None, ALU.mult).then_inc(ix_acc.sem, ix_acc.up())
                        dve_.wait_ge(ix_acc.sem, ix_acc.n)
                    else:
                        dve_.scalar_tensor_tensor(nb[:, i, 0:s], r, wh, nb[:, i, 0:s], ALU.mult, ALU.add).then_inc(ix_acc.sem, ix_acc.up())
                        dve_.wait_ge(ix_acc.sem, ix_acc.n)
                dve_.memset(nb[0:CH, i, s - CH:s], NEG).then_inc(own_v.sem, own_v.up())
                dve_.wait_ge(own_v.sem, own_v.n)
                for _ in range(TOPK // 8):
                    dve_.max(top, nb[:, i, 0:s]).then_inc(own_v.sem, own_v.up())
                    dve_.wait_ge(own_v.sem, own_v.n)
                    dve_.match_replace(nb[:, i, 0:s], top, nb[:, i, 0:s], TAKEN).then_inc(own_v.sem, own_v.up())
                    dve_.wait_ge(own_v.sem, own_v.n)
                dve_.tensor_scalar(nb[:, i, 0:s], nb[:, i, 0:s], TAKEN, NEG, ALU.is_gt, ALU.mult).then_inc(nb_ready.sem, nb_ready.up())

        pv_mm, pv_ev = sig("pv_mm"), sig("pv_ev")
        TILES_A, TILES_B, TILES_C, TILES_D = range(0, 4), range(4, 8), range(8, 12), range(12, 16)

        def values_pe(i, v_col, v_step):
            n = pv_mm.n
            if n >= 1:
                pe_.wait_ge(pv_ev.sem, n)
            for h in range(4):
                c = v_col + h * v_step
                for j in range(i + 1):
                    mm = pe_.matmul(PS[:, 6, h * 64:(h + 1) * 64], pT[:, j, h, :], proj[:, j, c:c + 64], start=j == 0, stop=j == i)
            mm.then_inc(pv_mm.sem, pv_mm.up())

        def y_of(t, g):
            base = (at(A_Q), at(B_Q), at(B_K), at(D_Q))[g]
            return proj[:, t, base:base + 256]

        rt_mm, rt_ev = sig("rt_mm"), sig("rt_ev")
        RB = (4, 0)

        def retention_pe():
            pe_.wait_ge(ix_relu.sem, 3 * IH)
            for i in range(NT):
                for j in range(i + 1):
                    n = rt_mm.n
                    if n >= 2:
                        pe_.wait_ge(rt_ev.sem, n - 1)
                    for h in range(4):
                        o, c = (h % 2) * 64, (h // 2) * P
                        mm = pe_.matmul(PS[:, RB[n % 2] + h % 2, c:c + P], TB[o:o + 64, 10 + h // 2, j * P:(j + 1) * P],
                                        TB[o:o + 64, 8 + h // 2, i * P:(i + 1) * P], start=True, stop=True)
                    mm.then_inc(rt_mm.sem, rt_mm.up())
                pe_.wait_ge(rt_ev.sem, rt_mm.n)
                values_pe(i, at(B_V), 64)

        def retention_dve():
            for i in range(NT):
                for j in range(i + 1):
                    n = rt_ev.n
                    dve_.wait_ge(rt_mm.sem, n + 1)
                    if j == 0 and i >= 1:
                        dve_.wait_ge(pv_mm.sem, i)
                    o = (i - j) * P
                    for r in range(2):
                        bank = PS[:, RB[n % 2] + r, 0:256].rearrange("p (h q) -> p h q", h=2)
                        mul = dve_.tensor_tensor(pT[:, j, r:4:2, :], bank, dtab[:, r:4:2, o:o + P], ALU.mult)
                    mul.then_inc(rt_ev.sem, rt_ev.up())
                dve_.wait_ge(pv_mm.sem, i + 1)
                dve_.tensor_copy(y_of(i, 1), PS[:, 6, 0:256]).then_inc(pv_ev.sem, pv_ev.up())

        pt = Turn(nc, ctx, f"pt_{l}", [PS[:, 4, :], PS[:, 5, :]], ident)

        def turn_probs_pe(i):
            for j in range(i + 1):
                pt.pe([(sm[:, h, j * P:(j + 1) * P], slice(h * P, (h + 1) * P)) for h in range(4)])

        def turn_probs_act(i):
            act_.wait_ge(pv_mm.sem, pt_tile[0])
            pt_tile[0] += 1
            for j in range(i + 1):
                bank = pt.bank(act_)
                act_.activation(PT[:, j * 512:(j + 1) * 512], bank, ACT.Copy).then_inc(pt.copied.sem, pt.copied.up())

        pt_tile = [4]
        at_mm, at_max, at_exp, at_rec = sig("at_mm"), sig("at_max"), sig("at_exp"), sig("at_rec")

        def attend_pe():
            pe_.wait_ge(ix_relu.sem, 3 * IH)
            for i in range(NT):
                s = (i + 1) * P
                for h in range(4):
                    if i >= 1:
                        pe_.wait_ge(at_max.sem, 4 * (i - 1) + h + 1)
                    o = (h % 2) * 64
                    pe_.matmul(PS[:, h, 0:s], TB[o:o + 64, h // 2, i * P:(i + 1) * P], TB[o:o + 64, 6, 0:s],
                               start=True, stop=True).then_inc(at_mm.sem, at_mm.up())
                pe_.wait_ge(at_exp.sem, 4 * (i + 1))
                turn_probs_pe(i)
                pe_.wait_ge(pt.copied.sem, pt.turned.n)
                values_pe(i, at(A_V), 0)

        def attend_dve():
            for i in range(NT):
                s = (i + 1) * P
                if i >= 1:
                    dve_.wait_ge(pt.turned.sem, sum(range(1, i + 1)))
                for h in range(4):
                    dve_.wait_ge(at_mm.sem, 4 * i + h + 1)
                    dve_.tensor_tensor_reduce(sm[:, h, 0:s], PS[:, h, 0:s], nb[:, i, 0:s], 1.0, -3e38, ALU.add, ALU.max,
                                              mx[:, h:h + 1]).then_inc(own_v.sem, own_v.up())
                    dve_.wait_ge(own_v.sem, own_v.n)
                    dve_.tensor_scalar(mx[:, h:h + 1], mx[:, h:h + 1], -0.125, None, ALU.mult).then_inc(at_max.sem, at_max.up())
                dve_.wait_ge(at_exp.sem, 4 * (i + 1))
                dve_.reciprocal(rec[:, 0:4], sumc[:, 0:4]).then_inc(own_v.sem, own_v.up())
                dve_.wait_ge(own_v.sem, own_v.n)
                dve_.wait_ge(pv_mm.sem, 4 + i + 1)
                y = y_of(i, 0).rearrange("p (h w) -> p h w", h=4)
                o = PS[:, 6, 0:256].rearrange("p (h w) -> p h w", h=4)
                dve_.tensor_tensor(y, o, rec[:, 0:4].rearrange("p (h w) -> p h w", w=1).to_broadcast([P, 4, 64]), ALU.mult).then_inc(pv_ev.sem, pv_ev.up())

        def attend_act():
            for i in range(NT):
                s = (i + 1) * P
                for h in range(4):
                    act_.wait_ge(at_max.sem, 4 * i + h + 1)
                    if h == 0 and i >= 1:
                        act_.wait_ge(pv_ev.sem, 4 + i)
                    act_.activation(sm[:, h, 0:s], sm[:, h, 0:s], ACT.Exp, scale=0.125, bias=mx[:, h:h + 1],
                                    accum_out=sumc[:, h:h + 1]).then_inc(at_exp.sem, at_exp.up())
                turn_probs_act(i)

        df_mm, df_max, df_exp, df_comb = sig("df_mm"), sig("df_max"), sig("df_exp"), sig("df_comb")
        DSC = float(np.float32(32.0 ** -0.5))
        second = NB[:, 1024:1536]
        TURNS_A = 10

        def diff_pe():
            pe_.wait_ge(at_max.sem, 4 * NT)
            for i in range(NT):
                s = (i + 1) * P
                for h in range(4):
                    n = df_mm.n
                    if n >= 2:
                        pe_.wait_ge(df_exp.sem, 2 * (n - 1))
                    for m in range(2):
                        o, b = ((2 * h + m) % 4) * 32, (2 * h + m) // 4
                        bank = 2 * (n % 2) + m
                        pe_.matmul(PS[:, bank, 0:s], TB[o:o + 32, b, i * P:(i + 1) * P], TB[o:o + 32, 2 + b, 0:s], start=True, stop=True,
                                   tile_position=(o, 0))
                        mm = pe_.matmul(PS[:, bank, s - CH:s], K[o:o + 1, K_NEG:K_NEG + P], K[o:o + 1, K_ONE:K_ONE + CH],
                                        start=False, stop=True, skip_group_check=True, tile_position=(o, 0))
                    mm.then_inc(df_mm.sem, df_mm.up())
                pe_.wait_ge(df_comb.sem, 4 * (i + 1))
                turn_probs_pe(i)
                pe_.wait_ge(pt.copied.sem, pt.turned.n)
                values_pe(i, at(D_V), 64)

        def diff_dve():
            dve_.wait_ge(lam_ready.sem, 1)
            for i in range(NT):
                s = (i + 1) * P
                for h in range(4):
                    n = 4 * i + h
                    dve_.wait_ge(df_mm.sem, n + 1)
                    b = 2 * (n % 2)
                    dve_.tensor_reduce(mx[:, b:b + 2], PS[:, b:b + 2, 0:s], AX.X, ALU.max).then_inc(own_v.sem, own_v.up())
                    dve_.wait_ge(own_v.sem, own_v.n)
                    dve_.tensor_scalar(mx[:, b:b + 2], mx[:, b:b + 2], -DSC, None, ALU.mult).then_inc(df_max.sem, df_max.up())
                    dve_.wait_ge(df_exp.sem, 2 * (n + 1))
                    c = rec[:, 4:5]
                    dve_.reciprocal(c, sumc[:, 2 * h + 1:2 * h + 2]).then_inc(own_v.sem, own_v.up())
                    dve_.wait_ge(own_v.sem, own_v.n)
                    dve_.tensor_scalar(c, c, sumc[:, 2 * h:2 * h + 1], lam[:, 3:4], ALU.mult, ALU.mult).then_inc(own_v.sem, own_v.up())
                    dve_.wait_ge(own_v.sem, own_v.n)
                    dve_.scalar_tensor_tensor(sm[:, h, 0:s], second[:, 0:s], c, sm[:, h, 0:s], ALU.mult, ALU.add).then_inc(df_comb.sem, df_comb.up())
                dve_.reciprocal(rec[:, 0:4], sumc[:, 0:8:2]).then_inc(own_v.sem, own_v.up())
                dve_.wait_ge(own_v.sem, own_v.n)
                dve_.wait_ge(pv_mm.sem, 8 + i + 1)
                y = y_of(i, 3).rearrange("p (h w) -> p h w", h=4)
                o = PS[:, 6, 0:256].rearrange("p (h w) -> p h w", h=4)
                dve_.tensor_tensor(y, o, rec[:, 0:4].rearrange("p (h w) -> p h w", w=1).to_broadcast([P, 4, 64]), ALU.mult).then_inc(pv_ev.sem, pv_ev.up())

        def diff_act():
            act_.wait_ge(pt.turned.sem, TURNS_A)
            for i in range(NT):
                s = (i + 1) * P
                if i >= 1:
                    act_.wait_ge(pv_ev.sem, 8 + i)
                    act_.wait_ge(pt.turned.sem, TURNS_A + sum(range(1, i + 1)))
                for h in range(4):
                    n = 4 * i + h
                    act_.wait_ge(df_max.sem, n + 1)
                    if n >= 1:
                        act_.wait_ge(df_comb.sem, n)
                    for m in range(2):
                        b = 2 * (n % 2) + m
                        dst = sm[:, h, 0:s] if m == 0 else second[:, 0:s]
                        act_.activation(dst, PS[:, b, 0:s], ACT.Exp, scale=DSC, bias=mx[:, b:b + 1],
                                        accum_out=sumc[:, 2 * h + m:2 * h + m + 1]).then_inc(df_exp.sem, df_exp.up())
                turn_probs_act(i)

        g_ex, g_exp, g_dec = sig("g_ex"), sig("g_exp"), sig("g_dec")
        kdT = Turn(nc, ctx, f"kd_{l}", [PS[:, 7, :]], ident)
        gs_mm, gs_ev, gd, gabs, ge, ga_mm, ga_ev = (sig(n) for n in ("gs_mm", "gs_ev", "gd", "gabs", "ge", "ga_mm", "ga_ev"))
        intra_mm = sig("intra_mm")
        b3 = bT.rearrange("p (c t) -> p c t", t=CH)
        gA = pT[:, 1, :, :]

        def gla_dve():
            dve_.wait_ge(df_comb.sem, 16)
            dve_.wait_ge(pv_ev.sem, 12)
            last = b3[:, :, CH - 1:CH]
            dve_.tensor_tensor(el.rearrange("p (c t) -> p c t", t=CH), last.to_broadcast([P, 8, CH]), b3, ALU.subtract).then_inc(g_ex.sem, g_ex.up())
            dve_.wait_ge(g_exp.sem, 3)
            dve_.tensor_tensor(qd, qT, eb, ALU.mult).then_inc(g_dec.sem, g_dec.up())
            dve_.tensor_tensor(kd, kT, el, ALU.mult).then_inc(g_dec.sem, g_dec.up())
            dve_.memset(states[0], 0.0).then_inc(own_v.sem, own_v.up())
            dve_.wait_ge(own_v.sem, own_v.n)
            for c in range(7):
                dve_.wait_ge(gs_mm.sem, c + 1)
                dve_.scalar_tensor_tensor(states[c + 1], states[c], gl8[:, c:c + 1], PS[:, 7, 0:256], ALU.mult, ALU.add).then_inc(gs_ev.sem, gs_ev.up())
                dve_.wait_ge(gs_ev.sem, gs_ev.n)
            for i in range(NT):
                if i >= 1:
                    dve_.wait_ge(ga_mm.sem, 7 * i)
                bt = bT[:, i * P:(i + 1) * P]
                for lev in range(LEVELS):
                    w = 2 << lev
                    v = bt.rearrange("p (n w) -> p n w", w=w)
                    o = SM[:, lev * P:(lev + 1) * P].rearrange("p (n w) -> p n w", w=w)
                    dve_.tensor_tensor(o, v, v[:, :, w // 2 - 1:w // 2].to_broadcast([P, P // w, w]), ALU.subtract).then_inc(gd.sem, gd.up())
                dve_.wait_ge(gabs.sem, i + 1)
                e6 = SM[:, 0:LEVELS * P].rearrange("p (n w) -> p n w", w=P)
                q6 = SM[:, 768:768 + LEVELS * P].rearrange("p (n w) -> p n w", w=P)
                qt = qT[:, i * P:(i + 1) * P].rearrange("p (n w) -> p n w", n=1).to_broadcast([P, LEVELS, P])
                kt = kT[:, i * P:(i + 1) * P].rearrange("p (n w) -> p n w", n=1).to_broadcast([P, LEVELS, P])
                dve_.tensor_tensor(q6, e6, qt, ALU.mult).then_inc(own_v.sem, own_v.up())
                dve_.wait_ge(own_v.sem, own_v.n)
                dve_.tensor_tensor(e6, e6, kt, ALU.mult).then_inc(ge.sem, ge.up())
                if i >= 1:
                    dve_.wait_ge(pv_mm.sem, 12 + i)
                for lev in range(LEVELS + 1):
                    n = ga_ev.n
                    dve_.wait_ge(ga_mm.sem, n + 1)
                    bank = PS[:, 4 * (n % 2):4 * (n % 2) + 4, 0:P]
                    if lev == 0:
                        m = ident.rearrange("p (n w) -> p n w", n=1).to_broadcast([P, 4, P])
                        dve_.tensor_tensor(gA, bank, m, ALU.mult).then_inc(ga_ev.sem, ga_ev.up())
                        dve_.wait_ge(ga_ev.sem, ga_ev.n)
                    else:
                        m = K[:, K_MASK + (lev - 1) * P:K_MASK + lev * P].bitcast(U32).rearrange("p (n w) -> p n w", n=1).to_broadcast([P, 4, P])
                        dve_.copy_predicated(gA, m, bank).then_inc(ga_ev.sem, ga_ev.up())
                        dve_.wait_ge(ga_ev.sem, ga_ev.n)
                dve_.wait_ge(intra_mm.sem, i + 1)
                dve_.tensor_copy(y_of(i, 2), PS[:, 6, 0:256]).then_inc(own_v.sem, own_v.up())
                dve_.wait_ge(own_v.sem, own_v.n)
                dve_.wait_ge(pv_mm.sem, 12 + i + 1)
                y = y_of(i, 2).rearrange("p (h w) -> p h w", h=4)
                dve_.tensor_tensor(y, y, PS[:, 0:4, 0:64], ALU.add).then_inc(pv_ev.sem, pv_ev.up())

        def gla_act():
            act_.wait_ge(g_ex.sem, 1)
            act_.activation(eb, bT, ACT.Exp).then_inc(g_exp.sem, g_exp.up())
            act_.activation(el, el, ACT.Exp).then_inc(g_exp.sem, g_exp.up())
            act_.activation(gl8.rearrange("p (c t) -> p c t", t=1), b3[:, :, CH - 1:CH], ACT.Exp).then_inc(g_exp.sem, g_exp.up())
            bank = kdT.bank(act_)
            act_.activation(PT[:, 0:512], bank, ACT.Copy).then_inc(kdT.copied.sem, kdT.copied.up())
            for i in range(NT):
                act_.wait_ge(gd.sem, LEVELS * (i + 1))
                act_.activation(SM[:, 0:768], SM[:, 0:768], ACT.Abs).then_inc(own_a.sem, own_a.up())
                act_.wait_ge(own_a.sem, own_a.n)
                act_.activation(SM[:, 0:768], SM[:, 0:768], ACT.Exp, scale=-1.0).then_inc(gabs.sem, gabs.up())

        def gla_pe():
            pe_.wait_ge(g_dec.sem, 2)
            kdT.pe([(kd[:, i * P:(i + 1) * P], slice(i * P, (i + 1) * P)) for i in range(NT)])
            pe_.wait_ge(kdT.copied.sem, 1)
            for c in range(7):
                o, i = (c % 2) * 64, c // 2
                if c >= 1:
                    pe_.wait_ge(gs_ev.sem, c)
                pe_.matmul(PS[:, 7, 0:256], pT[o:o + 64, 0, i, :], proj[o:o + 64, i, at(C_V):at(C_V) + 256], start=True, stop=True).then_inc(gs_mm.sem, gs_mm.up())
            for i in range(NT):
                pe_.wait_ge(ge.sem, i + 1)
                for lev in range(LEVELS + 1):
                    n = ga_mm.n
                    if n >= 2:
                        pe_.wait_ge(ga_ev.sem, n - 1)
                    if lev == 0:
                        pe_.wait_ge(pv_ev.sem, pv_mm.n)
                        pe_.wait_ge(gs_ev.sem, 7)
                    for h in range(4):
                        hp = slice(32 * h, 32 * h + 32)
                        if lev == 0:
                            a_, b_ = kT[hp, i * P:(i + 1) * P], qT[hp, i * P:(i + 1) * P]
                        else:
                            o = (lev - 1) * P
                            a_, b_ = SM[hp, o:o + P], SM[hp, 768 + o:768 + o + P]
                        mm = pe_.matmul(PS[:, 4 * (n % 2) + h, 0:P], a_, b_, start=True, stop=True, tile_position=(32 * h, 0))
                    mm.then_inc(ga_mm.sem, ga_mm.up())
                pe_.wait_ge(ga_ev.sem, ga_mm.n)
                for h in range(4):
                    cc = slice(h * 64, (h + 1) * 64)
                    mm = pe_.matmul(PS[:, 6, cc], gA[:, h, :], proj[:, i, at(C_V) + h * 64:at(C_V) + (h + 1) * 64],
                                    start=True, stop=True)
                mm.then_inc(intra_mm.sem, intra_mm.up())
                for h in range(4):
                    cc = slice(h * 64, (h + 1) * 64)
                    for c in (2 * i, 2 * i + 1):
                        o = (c % 2) * 64
                        mm = pe_.matmul(PS[o:o + 64, h, 0:64], qd[32 * h:32 * h + 32, c * CH:(c + 1) * CH],
                                        states[c][32 * h:32 * h + 32, cc], start=True, stop=True,
                                        tile_position=(32 * h, o))
                mm.then_inc(pv_mm.sem, pv_mm.up())

        sg_in, sg_e, vr_in, vr_out, y_ready = sig("sg_in"), sig("sg_e"), sig("vr_in"), sig("vr_out"), sig("y_ready")
        yT = Turn(nc, ctx, f"yT_{l}", [PS[:, 4, :], PS[:, 5, :]], ident)

        def heads_act():
            for t in range(NT):
                act_.wait_ge(sg_in.sem, 2 * (t + 1))
                act_.activation(SM[:, 0:512], SM[:, 0:512], ACT.Exp, scale=-1.0).then_inc(sg_e.sem, sg_e.up())
                act_.wait_ge(vr_in.sem, 4 * (t + 1))
                act_.activation(var, var, ACT.Ln, scale=1.0 / HD, bias=EPS).then_inc(own_a.sem, own_a.up())
                act_.wait_ge(own_a.sem, own_a.n)
                act_.activation(var, var, ACT.Exp, scale=-0.5).then_inc(vr_out.sem, vr_out.up())

        def heads_dve():
            dve_.wait_ge(ld_hng.sem, 16)
            dve_.tensor_scalar(HNG[:, 768:1024], HNG[:, 768:1024], 1.0 - lam_init, None, ALU.mult).then_inc(own_v.sem, own_v.up())
            dve_.wait_ge(own_v.sem, own_v.n)
            for t in range(NT):
                for n, col in enumerate((B_G, C_G)):
                    dve_.tensor_copy(SM[:, n * 256:(n + 1) * 256], proj[:, t, at(col):at(col) + 256]).then_inc(sg_in.sem, sg_in.up())
                ys = [y_of(t, g).rearrange("p (h w) -> p h w", h=4) for g in range(4)]

                def bc(a):
                    return a.rearrange("p (h w) -> p h w", w=1).to_broadcast([P, 4, 64])
                for g in (1, 2):
                    m = mean[:, 4 * g:4 * g + 4]
                    dve_.tensor_reduce(m, ys[g], AX.X, ALU.add).then_inc(own_v.sem, own_v.up())
                    dve_.wait_ge(own_v.sem, own_v.n)
                    dve_.tensor_scalar(m, m, 1.0 / HD, None, ALU.mult).then_inc(own_v.sem, own_v.up())
                    dve_.wait_ge(own_v.sem, own_v.n)
                    dve_.tensor_tensor(ys[g], ys[g], bc(m), ALU.subtract).then_inc(own_v.sem, own_v.up())
                    dve_.wait_ge(own_v.sem, own_v.n)
                for g in range(4):
                    sq = SM[:, 1024 + g * 256:1280 + g * 256]
                    dve_.tensor_tensor(sq.rearrange("p (h w) -> p h w", h=4), ys[g], ys[g], ALU.mult).then_inc(own_v.sem, own_v.up())
                    dve_.wait_ge(own_v.sem, own_v.n)
                    dve_.tensor_reduce(var[:, 4 * g:4 * g + 4], sq.rearrange("p (h w) -> p h w", h=4), AX.X, ALU.add).then_inc(vr_in.sem, vr_in.up())
                dve_.wait_ge(sg_e.sem, t + 1)
                s2 = SM[:, 0:512]
                dve_.tensor_scalar(s2, s2, 1.0, None, ALU.add).then_inc(own_v.sem, own_v.up())
                dve_.wait_ge(own_v.sem, own_v.n)
                dve_.reciprocal(s2, s2).then_inc(own_v.sem, own_v.up())
                dve_.wait_ge(own_v.sem, own_v.n)
                for n, col in enumerate((B_G, C_G)):
                    dve_.tensor_tensor(SM[:, n * 256:(n + 1) * 256], SM[:, n * 256:(n + 1) * 256],
                                       proj[:, t, at(col):at(col) + 256], ALU.mult).then_inc(own_v.sem, own_v.up())
                    dve_.wait_ge(own_v.sem, own_v.n)
                dve_.wait_ge(vr_out.sem, t + 1)
                for g in range(4):
                    dve_.tensor_tensor(ys[g], ys[g], bc(var[:, 4 * g:4 * g + 4]), ALU.mult).then_inc(own_v.sem, own_v.up())
                    dve_.wait_ge(own_v.sem, own_v.n)
                    o = dve_.tensor_tensor(y_of(t, g), y_of(t, g), HNG[:, g * 256:(g + 1) * 256], ALU.mult)
                    if g in (1, 2):
                        o.then_inc(own_v.sem, own_v.up())
                        dve_.wait_ge(own_v.sem, own_v.n)
                        o = dve_.tensor_tensor(y_of(t, g), y_of(t, g), SM[:, (g - 1) * 256:g * 256], ALU.mult)
                    o.then_inc(y_ready.sem, y_ready.up())
                    dve_.wait_ge(y_ready.sem, y_ready.n)

        def yT_pe():
            pe_.wait_ge(y_ready.sem, 4 * NT)
            for k in range(KD):
                yT.pe([(y_of(t, k // 2)[:, (k % 2) * P:(k % 2 + 1) * P], slice(t * P, (t + 1) * P)) for t in range(NT)])
            pe_.wait_ge(yT.copied.sem, KD)

        def yT_act():
            for k in range(KD):
                bank = yT.bank(act_)
                act_.activation(hT[:, k, :], bank, ACT.Copy).then_inc(yT.copied.sem, yT.copied.up())

        class Back:
            def __init__(self, name, g):
                self.g = g
                self.mm, self.sq, self.sum, self.rs, self.added = (sig(name + s) for s in ("_mm", "_sq", "_sum", "_rs", "_added"))

            def pe(self, src, n_tiles):
                def one(w, m, k, t, half):
                    return product(PS[:, 2 * t + half, :], src[:, 4 * m + k, t * P:(t + 1) * P],
                                   w[:, k, half * 512:(half + 1) * 512], start=m == 0 and k == 0,
                                   stop=m == n_tiles - 1 and k == 3)
                for m in range(n_tiles - 1):
                    w = take()
                    for k in range(4):
                        for t in range(NT):
                            for half in range(2):
                                one(w, m, k, t, half)
                w = take()
                for t in range(NT):
                    for k in range(4):
                        for half in range(2):
                            mm = one(w, n_tiles - 1, k, t, half)
                    mm.then_inc(self.mm.sem, self.mm.up())

            def squares(self, t):
                act_.wait_ge(self.mm.sem, t + 1)
                for half in range(2):
                    n = 2 * t + half
                    if n >= 2:
                        act_.wait_ge(self.sq.sem, n - 1)
                    act_.activation(SM[:, half * 512:half * 512 + 512], PS[:, n, :], ACT.Square,
                                    accum_out=ms[:, n:n + 1]).then_inc(self.sq.sem, self.sq.up())

            def rsqrt(self, t):
                act_.wait_ge(self.sum.sem, t + 1)
                r_ = rs[:, t:t + 1]
                act_.activation(r_, r_, ACT.Ln, scale=1.0 / D, bias=EPS).then_inc(own_a.sem, own_a.up())
                act_.wait_ge(own_a.sem, own_a.n)
                act_.activation(r_, r_, ACT.Exp, scale=-0.5).then_inc(self.rs.sem, self.rs.up())

            def act(self):
                for t in range(NT):
                    self.squares(t)
                    if t:
                        self.rsqrt(t - 1)
                self.rsqrt(NT - 1)

            def sums(self, t):
                dve_.wait_ge(self.sq.sem, 2 * (t + 1))
                dve_.tensor_tensor(rs[:, t:t + 1], ms[:, 2 * t:2 * t + 1], ms[:, 2 * t + 1:2 * t + 2], ALU.add).then_inc(self.sum.sem, self.sum.up())

            def dve(self):
                dve_.wait_ge(gates_ready.sem, 1)
                self.sums(0)
                for t in range(NT):
                    if t + 1 < NT:
                        self.sums(t + 1)
                    dve_.wait_ge(self.rs.sem, t + 1)
                    for half in range(2):
                        c = slice(half * 512, (half + 1) * 512)
                        g = slice(self.g * D + half * 512, self.g * D + (half + 1) * 512)
                        dve_.scalar_tensor_tensor(xn[:, t, c], PS[:, 2 * t + half, :], rs[:, t:t + 1], GR[:, g], ALU.mult, ALU.mult).then_inc(own_v.sem, own_v.up())
                    dve_.wait_ge(own_v.sem, own_v.n)
                    dve_.tensor_tensor(x3[:, t, :], x3[:, t, :], xn[:, t, :], ALU.add).then_inc(self.added.sem, self.added.up())

        tail = AR[:, NFF * T:]
        if next_mod is not None:
            nxt = Modulation(nc, ctx, f"next_{l}", [(next_mod_w, csc)],
                             [v[:, 0:2048].rearrange("p (k n) -> p k n", k=KD) for v in (PT, NB, tail)],
                             [QD[:, r * 512:(r + 1) * 512] for r in range(2)],
                             [GL[0:1, r * 512:(r + 1) * 512] for r in range(2)], PS[0:1, 7, :], ones_col, next_mod)
        NEXT_FROM, NEXT_STEP = 6, 2

        def next_after(m):
            return next_mod is not None and m >= NEXT_FROM and (m - NEXT_FROM) % NEXT_STEP == 0 and (m - NEXT_FROM) // NEXT_STEP < nxt.tiles

        f_mm, f_relu, f_ready = sig("f_mm"), sig("f_relu"), sig("f_ready")

        def mlp_pe():
            for m in range(NFF):
                if m % 4 == 0:
                    w = take()
                c = m % 4
                if m >= 4:
                    pe_.wait_ge(f_relu.sem, m - 3)
                for k in range(KD):
                    mm = product(PS[:, c, :], w[:, k, c * P:(c + 1) * P], hT[:, k, :], start=k == 0, stop=k == KD - 1)
                mm.then_inc(f_mm.sem, f_mm.up())
                if next_after(m):
                    nxt.pe()
            pe_.wait_ge(f_ready.sem, NFF)
            if next_mod is not None:
                pe_.wait_ge(nxt.copied.sem, nxt.tiles)

        def mlp_act():
            for m in range(NFF):
                act_.wait_ge(f_mm.sem, m + 1)
                if m >= 2:
                    act_.wait_ge(f_ready.sem, m - 1)
                act_.activation(relu2[m % 2], PS[:, m % 4, :], ACT.Relu).then_inc(f_relu.sem, f_relu.up())
                if next_after(m):
                    nxt.act()

        def mlp_dve():
            for m in range(NFF):
                dve_.wait_ge(f_relu.sem, m + 1)
                dve_.tensor_tensor(fT[:, m, :], relu2[m % 2], relu2[m % 2], ALU.mult).then_inc(f_ready.sem, f_ready.up())
                if next_after(m + 2):
                    nxt.dve()
                    nxt.dve()

        back1 = Back("attn", 0)
        norm1 = Normed("n1", 8, 0, ld_x, 0)
        norm2 = Normed("n2", 32, 24, back1.added, 1)
        back2 = Back("mlp", 1)

        block = ctx.enter_context(nc.Block())

        @block.sync
        def _(sp):
            loads_sp(sp)
            for n in range(len(tiles)):
                if n >= RING:
                    sp.wait_ge(w_used.sem, n - RING + 1)
                sp.dma_start(slot(n), tiles[n]).then_inc(w_loaded[n % RING].sem, w_loaded[n % RING].up(16))
            sp.wait_ge(back2.added.sem, NT)
            sp.dma_start(x_out.rearrange("(t p) d -> p t d", p=P), x3).then_inc(stored.sem, stored.up(16))
            sp.wait_ge(stored.sem, 16)

        @block.gpsimd
        def _(pool):
            pool.wait_ge(b_ready.sem, 1)
            pool.wait_ge(gates_ready.sem, 1)
            rope(pool_, ROPE_BD, rope_bd, own_g, NB)
            dup_pool()
            if next_mod is not None:
                pool.wait_ge(back1.added.sem, NT)
                pool.wait_ge(silu.sem, 2)
                for n in range(2 * nxt.tiles):
                    nxt.load(n)

        @block.tensor
        def _(pe):
            cond_pe()
            lam_pe()
            pe.wait_ge(lam_ready.sem, 1)
            norm1.pe()
            proj_pe()
            pe.wait_ge(rope_a.sem, 4 * NT)
            qk_pe(0, 6)
            pe.wait_ge(dup.sem, 4)
            qk_pe(6, 8)
            index_pe()
            pe.wait_ge(rope_bd.sem, 4 * NT)
            qk_pe(8, 12)
            pe.wait_ge(qk.copied.sem, 12)
            retention_pe()
            pe.wait_ge(nb_ready.sem, NT)
            attend_pe()
            pe.wait_ge(pv_ev.sem, 8)
            qk_pe(12, 16)
            pe.wait_ge(qk.copied.sem, 16)
            diff_pe()
            gla_pe()
            yT_pe()
            pe.wait_ge(pv_ev.sem, 16)
            back1.pe(hT, 2)
            pe.wait_ge(back1.added.sem, NT)
            norm2.pe()
            mlp_pe()
            back2.pe(fT, 8)

        @block.scalar
        def _(act):
            if next_mod is not None:
                cond_act()
            lam_act()
            trig_act()
            norm1.act()
            proj_act()
            qk_act(0, 8)
            index_act()
            qk_act(8, 12)
            attend_act()
            act.wait_ge(at_max.sem, 4 * NT)
            qk_act(12, 16)
            diff_act()
            gla_act()
            heads_act()
            yT_act()
            back1.act()
            norm2.act()
            mlp_act()
            back2.act()
            if next_mod is not None:
                nxt.wait_stored(act)

        @block.vector
        def _(dve):
            cond_dve()
            mod_dve()
            lam_dve()
            trig_dve()
            norm1.dve()
            gates_dve()
            decay_dve()
            rope(dve_, ROPE_A, rope_a, own_v, SM[:, 1024:2048])
            index_dve()
            retention_dve()
            attend_dve()
            diff_dve()
            gla_dve()
            heads_dve()
            back1.dve()
            norm2.dve()
            mlp_dve()
            back2.dve()


def program(nc, a, out, consts_a, consts_b, consts_c):
    x1, x2, x3 = (nc.dram_tensor(name, [T, D], F32).ap() for name in ("x_mixed", "x_block1", "x_layer1"))
    mod_later = nc.dram_tensor("mod_later", [9 * D], F32).ap()
    mod_next = nc.dram_tensor("mod_next", [6 * D], F32).ap()
    mixers(nc, a["x"][0], x1, a["c"][0], a["ctx"][0], a["c_ctx"], a["w_mod"][0], a["b_mod"][0], a["g_mix"][0], a["w_in"][0],
           a["w_out"][0], a["dn_conv_w"][0], a["dn_a_log"][0], a["dn_dt_bias"][0], a["dn_norm_g"][0], a["cf_dw_w"][0],
           a["cf_dw_b"][0], a["cf_ln_g"][0], a["cf_ln_b"][0],
           a["c_2"][0], a["mod_w_2"][0], mod_later, consts_a)
    moe(nc, x1, x2, mod_later[0:3 * D], a["b_mod"][0], a["g_ffn"][0], a["router_w"][0], a["router_bias"][0],
        a["exp_w_gate"][0], a["exp_w_up"][0], a["exp_w_down"][0], a["sh_w_gate"][0], a["sh_w_up"][0], a["sh_w_down"][0],
        a["g_final"], consts_b)
    for l, (src, dst) in enumerate(((x2, x3), (x3, out[0]))):
        per_layer = [a[name + "_2"][l] for name in (
            "mod_b", "attn_pre_g", "attn_post_g", "mlp_pre_g", "mlp_post_g", "w_in", "gla_wa2", "gla_ba",
            "lam_q1", "lam_k1", "lam_q2", "lam_k2", "head_norm_g", "w_out", "mlp_w1", "mlp_w2")]
        mods = (mod_later[3 * D:], a["mod_w_2"][1], mod_next) if l == 0 else (mod_next, None, None)
        layer(nc, l, src, dst, a["c_2"][0], a["positions_2"][0], *mods, *per_layer, consts_c)


def kernel(**inputs):
    import concourse.bacc as bacc
    from concourse.bass_utils import run_bass_kernel_spmd

    nc = bacc.Bacc("TRN2", target_bir_lowering=False, num_devices=1)
    arrays = {f"in_{name}": np.ascontiguousarray(value) for name, value in inputs.items()}
    arrays["consts_mixers"], arrays["consts_moe"], arrays["consts_layer"] = mixer_constants(), moe_constants(), layer_constants()
    aps = {name: nc.dram_tensor(name, a.shape, mybir.dt.from_np(a.dtype), kind="ExternalInput").ap() for name, a in arrays.items()}
    out = nc.dram_tensor("out", (1, T, D), F32, kind="ExternalOutput").ap()
    program(nc, {name: aps[f"in_{name}"] for name in inputs}, out, aps["consts_mixers"], aps["consts_moe"], aps["consts_layer"])
    r = run_bass_kernel_spmd(nc, [arrays], core_ids=[0])
    return r.results[0]["out"]
```
